# Optimizing a Trainium2 kernel written in Bass

```python
import jax, jax.numpy as jnp
from jax import lax
import numpy as np

D_MODEL = 1024
BATCH = 1
SEQ = 512
DEPTH = 1
DEC_BATCH = 8
DEC_SEQ = 4
PAST_LEN = 4096
PAGE_SIZE = 128

D_CONV = D_MODEL
CONV_WIDTH = 31
CONV_BUF = CONV_WIDTH - 1
M_HEADS = 4
D_M = 2 * D_MODEL
DV = D_M // M_HEADS
DK = DV // 2
D_QK = M_HEADS * DK
D_FF = 4 * D_MODEL
CHUNK = 128
EPS = 1e-6
FGATE_BIAS_INIT = 3.0
IN_SIZES = (D_CONV, D_CONV, D_QK, D_QK, D_M, D_M, M_HEADS, M_HEADS, D_MODEL, D_MODEL)
D_IN = sum(IN_SIZES)

kernel_name = "conformer_mlstm_gated_hybrid_step"

def rmsnorm(x, g):
    xf = x.astype(jnp.float32)
    y = xf * lax.rsqrt(jnp.mean(xf * xf, axis=-1, keepdims=True) + EPS)
    return (y * g.astype(jnp.float32)).astype(x.dtype)

def layernorm(x, g, b):
    xf = x.astype(jnp.float32)
    mu = jnp.mean(xf, axis=-1, keepdims=True)
    xc = xf - mu
    y = xc * lax.rsqrt(jnp.mean(xc * xc, axis=-1, keepdims=True) + EPS)
    return (y * g.astype(jnp.float32) + b.astype(jnp.float32)).astype(x.dtype)

def split_in(proj):
    idx = []
    acc = 0
    for s in IN_SIZES[:-1]:
        acc += s
        idx.append(acc)
    return jnp.split(proj, idx, axis=-1)

def mlstm_scan(q, k, v, ig, lf, C0, n0, m0):
    B, T = q.shape[0], q.shape[1]
    L = min(CHUNK, T)
    NC = T // L
    mask = jnp.tril(jnp.ones((L, L), dtype=bool))

    def chunks(a):
        return jnp.moveaxis(a.reshape((B, NC, L) + a.shape[2:]), 1, 0)

    def step(carry, xs):
        C, n, m = carry
        qc, kc, vc, ic, fc = xs
        b = jnp.cumsum(fc, axis=1)
        D = b[:, :, None, :] - b[:, None, :, :] + ic[:, None, :, :]
        D = jnp.where(mask[None, :, :, None], D, -jnp.inf)
        inter = b + m[:, None, :]
        m_t = jnp.maximum(inter, jnp.max(D, axis=2))
        w_intra = jnp.exp(D - m_t[:, :, None, :])
        w_inter = jnp.exp(inter - m_t)
        s = jnp.einsum('bthk,bshk->btsh', qc, kc) * w_intra
        num = jnp.einsum('btsh,bshv->bthv', s, vc) + w_inter[..., None] * jnp.einsum('bhvk,bthk->bthv', C, qc)
        den = jnp.sum(s, axis=2) + w_inter * jnp.einsum('bhk,bthk->bth', n, qc)
        h = num / jnp.maximum(jnp.abs(den), jnp.exp(-m_t))[..., None]
        bL = b[:, -1]
        dL = bL[:, None, :] - b + ic
        m_new = jnp.maximum(bL + m, jnp.max(dL, axis=1))
        wk = jnp.exp(dL - m_new[:, None, :])
        dec = jnp.exp(bL + m - m_new)
        C_new = dec[..., None, None] * C + jnp.einsum('bsh,bshv,bshk->bhvk', wk, vc, kc)
        n_new = dec[..., None] * n + jnp.einsum('bsh,bshk->bhk', wk, kc)
        return (C_new, n_new, m_new), h

    (C, n, m), h = lax.scan(step, (C0, n0, m0),
                            (chunks(q), chunks(k), chunks(v), chunks(ig), chunks(lf)))
    h = jnp.moveaxis(h, 0, 1).reshape(B, T, M_HEADS, DV)
    return h, C, n, m

def trunk_layer(x, conv_buf, C0, n0, m0, g_pre_mix, w_in, b_in, w_dw, b_dw, g_cln, b_cln,
                w_conv_out, g_mh, w_m_out, w_o, g_post_mix, g_pre_ff, w_ff1, b_ff1, w_ff2, b_ff2,
                g_post_ff):
    B, T, _ = x.shape
    f32 = jnp.float32
    h = rmsnorm(x, g_pre_mix)
    proj = jnp.einsum('btd,de->bte', h, w_in) + b_in
    u_a, u_g, q, k, v, o, ig, fg, gate_conv, gate_m = split_in(proj)

    u = u_a * jax.nn.sigmoid(u_g)
    full = jnp.concatenate([conv_buf.astype(u.dtype), u], axis=1)
    c = lax.conv_general_dilated(full, w_dw[:, None, :], window_strides=(1,), padding='VALID',
                                 dimension_numbers=('NWC', 'WIO', 'NWC'),
                                 feature_group_count=D_CONV) + b_dw
    c = jax.nn.silu(layernorm(c, g_cln, b_cln))
    y_conv = jnp.einsum('btc,cd->btd', c, w_conv_out)
    new_buf = full[:, -CONV_BUF:]

    qh = q.reshape(B, T, M_HEADS, DK).astype(f32) * (DK ** -0.5)
    kh = k.reshape(B, T, M_HEADS, DK).astype(f32)
    vh = v.reshape(B, T, M_HEADS, DV).astype(f32)
    hm, C, n, m = mlstm_scan(qh, kh, vh, ig.astype(f32), jax.nn.log_sigmoid(fg.astype(f32)),
                             C0.astype(f32), n0.astype(f32), m0.astype(f32))
    hm = hm * lax.rsqrt(jnp.mean(hm * hm, axis=-1, keepdims=True) + EPS) \
        * g_mh.reshape(M_HEADS, DV).astype(f32)
    hm = hm.reshape(B, T, D_M).astype(x.dtype) * jax.nn.sigmoid(o)
    y_m = jnp.einsum('btm,md->btd', hm, w_m_out)

    mix = jax.nn.sigmoid(gate_conv) * y_conv + jax.nn.sigmoid(gate_m) * y_m
    x = x + rmsnorm(jnp.einsum('btd,de->bte', mix, w_o), g_post_mix)

    hf = rmsnorm(x, g_pre_ff)
    ff = jnp.einsum('btf,fd->btd', jnp.square(jax.nn.relu(jnp.einsum('btd,df->btf', hf, w_ff1) + b_ff1)), w_ff2) + b_ff2
    x = x + rmsnorm(ff, g_post_ff)
    return x, new_buf, C, n, m

def setup_inputs(seed: int = 0) -> dict:
    key = jax.random.key(seed)
    ks = jax.random.split(key, 32)
    nrm = jax.random.normal
    f32 = jnp.float32
    x_prompt = nrm(ks[0], (BATCH, SEQ, D_MODEL), f32)
    x_sample = nrm(ks[1], (DEC_BATCH, DEC_SEQ, D_MODEL), f32)
    state_conv = nrm(ks[2], (DEPTH, DEC_BATCH, CONV_BUF, D_CONV), f32)
    state_C = 0.1 * nrm(ks[3], (DEPTH, DEC_BATCH, M_HEADS, DV, DK), f32)
    state_n = 0.5 * nrm(ks[4], (DEPTH, DEC_BATCH, M_HEADS, DK), f32)
    state_m = nrm(ks[5], (DEPTH, DEC_BATCH, M_HEADS), f32)

    def gain(k, n):
        return 1.0 + 0.05 * nrm(k, (DEPTH, n), f32)

    f_start = sum(IN_SIZES[:7])
    b_in = 0.02 * nrm(ks[8], (DEPTH, D_IN), f32)
    b_in = b_in.at[:, f_start:f_start + M_HEADS].add(FGATE_BIAS_INIT)
    return {
        "x_prompt": x_prompt,
        "x_sample": x_sample,
        "state_conv": state_conv,
        "state_C": state_C,
        "state_n": state_n,
        "state_m": state_m,
        "g_pre_mix": gain(ks[6], D_MODEL),
        "w_in": nrm(ks[7], (DEPTH, D_MODEL, D_IN), f32) * D_MODEL ** -0.5,
        "b_in": b_in,
        "w_dw": nrm(ks[9], (DEPTH, CONV_WIDTH, D_CONV), f32) * CONV_WIDTH ** -0.5,
        "b_dw": 0.02 * nrm(ks[10], (DEPTH, D_CONV), f32),
        "g_cln": gain(ks[11], D_CONV),
        "b_cln": 0.02 * nrm(ks[12], (DEPTH, D_CONV), f32),
        "w_conv_out": nrm(ks[13], (DEPTH, D_CONV, D_MODEL), f32) * D_CONV ** -0.5,
        "g_mh": gain(ks[14], D_M),
        "w_m_out": nrm(ks[15], (DEPTH, D_M, D_MODEL), f32) * D_M ** -0.5,
        "w_o": nrm(ks[16], (DEPTH, D_MODEL, D_MODEL), f32) * D_MODEL ** -0.5,
        "g_post_mix": gain(ks[17], D_MODEL),
        "g_pre_ff": gain(ks[18], D_MODEL),
        "w_ff1": nrm(ks[19], (DEPTH, D_MODEL, D_FF), f32) * D_MODEL ** -0.5,
        "b_ff1": 0.02 * nrm(ks[20], (DEPTH, D_FF), f32),
        "w_ff2": nrm(ks[21], (DEPTH, D_FF, D_MODEL), f32) * D_FF ** -0.5,
        "b_ff2": 0.02 * nrm(ks[22], (DEPTH, D_MODEL), f32),
        "g_post_ff": gain(ks[23], D_MODEL),
    }

def reference(x_prompt, x_sample, state_conv, state_C, state_n, state_m,
              g_pre_mix, w_in, b_in, w_dw, b_dw, g_cln, b_cln, w_conv_out, g_mh, w_m_out,
              w_o, g_post_mix, g_pre_ff, w_ff1, b_ff1, w_ff2, b_ff2, g_post_ff):
    f32 = jnp.float32
    Bp = x_prompt.shape[0]
    yp, ys = x_prompt, x_sample
    cp_l, Cp_l, np_l, mp_l = [], [], [], []
    cs_l, Cs_l, ns_l, ms_l = [], [], [], []
    for d in range(DEPTH):
        prm = (g_pre_mix[d], w_in[d], b_in[d], w_dw[d], b_dw[d], g_cln[d], b_cln[d],
               w_conv_out[d], g_mh[d], w_m_out[d], w_o[d], g_post_mix[d], g_pre_ff[d],
               w_ff1[d], b_ff1[d], w_ff2[d], b_ff2[d], g_post_ff[d])
        buf0 = jnp.zeros((Bp, CONV_BUF, D_CONV), x_prompt.dtype)
        C0 = jnp.zeros((Bp, M_HEADS, DV, DK), f32)
        n0 = jnp.zeros((Bp, M_HEADS, DK), f32)
        m0 = jnp.zeros((Bp, M_HEADS), f32)
        yp, bp, Cp, npn, mp = trunk_layer(yp, buf0, C0, n0, m0, *prm)
        cp_l.append(bp); Cp_l.append(Cp); np_l.append(npn); mp_l.append(mp)
        ys, bs, Cs, nsn, ms = trunk_layer(ys, state_conv[d], state_C[d], state_n[d], state_m[d], *prm)
        cs_l.append(bs.astype(state_conv.dtype)); Cs_l.append(Cs.astype(state_C.dtype))
        ns_l.append(nsn.astype(state_n.dtype)); ms_l.append(ms.astype(state_m.dtype))
    return (yp, ys,
            jnp.stack(cp_l), jnp.stack(Cp_l), jnp.stack(np_l), jnp.stack(mp_l),
            jnp.stack(cs_l), jnp.stack(Cs_l), jnp.stack(ns_l), jnp.stack(ms_l))


_drawn_inputs = setup_inputs


def setup_inputs(seed=0):
    import zlib

    import numpy as np

    out = dict(_drawn_inputs(seed))
    spreads = {}
    factors = {'b_cln': 5.042, 'b_ff1': 4.228, 'b_ff2': 6.01}
    for name, (base, spread) in spreads.items():
        noise = np.random.default_rng([zlib.crc32(name.encode()), seed]).standard_normal(out[name].shape)
        drawn = base * np.exp(spread * noise) if base else spread * noise
        out[name] = __import__('jax').numpy.asarray(drawn.astype(out[name].dtype))
    for name, factor in factors.items():
        out[name] = (out[name] * factor).astype(out[name].dtype)
    return out
```

```python
import concourse.bass as bass
from concourse import mybir
from contextlib import ExitStack

P = 128
D_MODEL = 1024
KT = D_MODEL // P
SEQ = 512
DEC_B, DEC_T = 8, 4
NS = DEC_B * DEC_T
TT = SEQ + NS
HALF = TT // 2
WIDTH = 31
HIST = WIDTH - 1
SROW = HIST + DEC_T
UCOLS = HIST + SEQ + DEC_B * SROW
HEADS = 4
DV, DK = 512, 256
VT, QT = DV // P, DK // P
ST = SEQ // P
EPS = 1e-6
CHUNK = KT * P
RING = 4
C_RING = 4
HID = 16
PERHEAD = 2 * QT + 2 * VT

C_GLU = 0
C_HEAD = C_GLU + 2 * KT
C_GATE = C_HEAD + HEADS * PERHEAD
C_CONV = C_GATE + 2 * KT
C_MEM = C_CONV + KT
C_OUT = C_MEM + 2 * KT
C_FF = C_OUT + KT
PERHALF = HID + 2 * KT
N_CHUNKS = C_FF + 2 * PERHALF

USES = ["q0", "q1", "k0", "k1", "v0", "kts", "v1", "v2", "v3", "v4",
        "o0", "cu0", "cu1", "o1", "cu2", "cu3", "o2", "cu4", "cu5", "o3", "cu6", "cu7",
        "pv0", "pv1", "pv2", "pv3", "cc01", "cc23"]
USES_HEAD = len(USES) // 2
BY_CHUNK = {"q0": 0, "q1": 1, "k0": 2, "k1": 3, "v4": 7, "o0": 8, "o1": 9, "o2": 10, "o3": 11}
BY_SLOT = [[n for n in USES[s::2] if n not in BY_CHUNK] for s in range(2)]
S_HEAD = KT
S_GATE = S_HEAD + HEADS * USES_HEAD
S_CONV = S_GATE + KT
S_MEM = S_CONV + KT // 2
S_OUT = S_MEM + KT // 2
S_FF = S_OUT + KT // 2
S_HALF = HID // 2 + KT // 2

COLS = {}
_at = 0
for _name, _n in (("b_ug", 8), ("b_ua", 8), ("b_q", 8), ("b_k", 8), ("b_o", 16), ("b_gc", 8), ("b_gm", 8),
                  ("b_dw", 8), ("g_cln", 8), ("b_cln", 8), ("g_pre_mix", 8), ("g_mh", 16), ("g_post_mix", 8),
                  ("g_pre_ff", 8), ("b_ff1", 32), ("b_ff2", 8), ("g_post_ff", 8)):
    COLS[_name] = _at
    _at += _n
N_COLS = _at

R_NEGM, R_M, R_WINTER, R_WK, R_DEC = 0, TT, 2 * TT, 2 * TT + NS, 2 * TT + 2 * NS
N_ROW = R_DEC + DEC_B

PT_AT = [0, 512, 896, 1152, 1280]
N_PT = 1280 + NS
ST_AT = [(0, 0), (1, 0), (2, 0), (1, 384), (2, 256)]


V_TAPS = [(4, 5), (5, 7), (7, 9), (9, 12)]
C_TAPS = [(12, 14), (14, 14), (14, 16), (16, 18), (18, 20), (20, 22), (22, 24), (24, 27)]
DVE_PER_HEAD = 146


class Steps:

    def __init__(self):
        self.n, self.off = 0, 0

    def loop(self, i, per):
        self.start, self.per, self.off = self.n, per, i * per

    def leave(self, turns):
        assert self.n - self.start == self.per, (self.n - self.start, self.per)
        self.n, self.off = self.start + self.per * turns, 0

    def add(self):
        self.n += 1
        return self.off + self.n


def hybrid_layer(nc, xT, wstream, w_gates, cols, b_gates, b_v, w_dw, hist, c_in, n_in, m_in,
                 yT, conv_p, conv_s, c_p, n_p, m_p, c_s, n_s, m_s):
    f32, f32r = mybir.dt.float32, mybir.dt.float32r
    ALU = mybir.AluOpType
    ACT = mybir.ActivationFunctionType
    X = mybir.AxisListType.X
    rows_dram = nc.dram_tensor("head_rows", (HEADS, N_ROW), f32, kind="Internal").ap()

    ctx = ExitStack()
    with ctx:
        cursor = [4224]

        def at(name, shape, dt, where=None):
            size = 4
            for n in shape[1:]:
                size *= n
            size = (size + 31) // 32 * 32
            where_ = cursor[0] if where is None else where
            t = nc.alloc_sbuf_tensor_at(name, shape, dt, offset=where_)
            if where is None:
                cursor[0] += size
            assert max(cursor[0], where_ + size) <= 229344, (name, cursor[0])
            return t

        wraw = at("wraw", [P, 2, KT, P], f32)
        whi = at("whi", [P, RING, KT, P], f32r)
        wlo = at("wlo", [P, RING, KT, P], f32r)
        col = at("col", [P, N_COLS], f32)
        wdw = at("wdw", [P, KT, WIDTH], f32)
        ones = at("ones", [P, P], f32)
        ident = at("ident", [P, P], f32)
        causal = at("causal", [P, P], f32)
        causal_s = at("causal_s", [NS, DEC_B, DEC_T], f32)
        own = at("own", [NS, DEC_B], f32)
        nold = at("nold", [P, HEADS, QT, DEC_B], f32)
        nnew = at("nnew", [P, HEADS, QT, DEC_B], f32)
        npn = at("npn", [P, HEADS, QT], f32)
        eps = at("eps", [P, 1], f32)
        acol = at("acol", [P, ST + 1, HEADS], f32)
        wkcol = at("wkcol", [NS, HEADS], f32)
        mcol = at("mcol", [NS, HEADS], f32)
        xa0 = cursor[0]
        ahi = at("ahi", [P, KT, TT], f32r)
        alo = at("alo", [P, KT, TT], f32r)
        mhi = at("mhi", [P, 2 * KT, TT], f32r, xa0)
        hm0 = cursor[0]
        hm = at("hm", [P, 2 * KT, TT], f32)
        mlo = at("mlo", [P, 2 * KT, TT], f32r, hm0)
        x0 = at("x0", [P, KT, TT], f32, hm0)
        g0 = hm0 + KT * TT * 4
        wg = at("wg", [P, KT, 36], f32, g0)
        wghi = at("wghi", [P, KT, 36], f32r, g0 + KT * 36 * 4)
        wglo = at("wglo", [P, KT, 36], f32r, g0 + 2 * KT * 36 * 4)
        hidhi = at("hidhi", [P, HID, TT], f32r, hm0)
        u0 = cursor[0]
        u = at("u", [P, KT, UCOLS], f32)
        y = at("y", [P, KT, TT], f32, u0)
        tmp0 = cursor[0]
        vtok = at("vtok", [P, ST + 1, DV], f32)
        pt = at("pt", [P, N_PT], f32)
        kw = at("kw", [P, ST, DK], f32)
        hs0 = cursor[0]
        hs = at("hs", [NS, DV], f32)
        kwh = at("kwh", [NS, DK], f32r, hs0)
        kwl = at("kwl", [NS, DK], f32, hs0 + DK * 4)
        kws = at("kws", [NS, DK], f32, cursor[0])
        hsq = at("hsq", [NS, DV], f32)
        qT = at("qT", [P, QT, TT], f32)
        kT = at("kT", [P, QT, TT], f32)
        hb = at("hb", [P, N_ROW], f32)
        wkp = at("wkp", [P, ST], f32)
        bv = at("bv", [P, DV], f32, cursor[0])
        hr = at("hr", [P, 2, SEQ], f32)
        sg = at("sg", [P, TT], f32, cursor[0])
        sqh = at("sqh", [P, 2, SEQ], f32)
        sqacc = at("sqacc", [P, SEQ], f32)
        rden = at("rden", [P, SEQ], f32)
        qm = at("qm", [P, QT, DEC_B * 36], f32)
        qn = at("qn", [P, QT, NS], f32)
        kn = at("kn", [P, QT, NS], f32)
        nd = at("nd", [P, QT, DEC_B], f32)
        kr = at("kr", [P, QT, DEC_B], f32)
        cst = at("cst", [P, VT, DK], f32, cursor[0])
        kst = at("kst", [96, DEC_B, DK], f32r)
        vst = at("vst", [96, DV], f32r)
        sst = at("sst", [NS, 8], f32)
        accp = at("accp", [P, 2, SEQ], f32)
        accs = at("accs", [P, 2, NS], f32)
        crg = at("crg", [P, C_RING, QT, DV], f32)
        rw = tmp0
        row = {}
        for name in ("ig", "fg", "ex", "B", "a", "M", "one"):
            row[name] = at("row_" + name, [HEADS, TT], f32, rw)
            rw += TT * 4
        rout = at("rout", [HEADS, N_ROW], f32, rw)
        rw += N_ROW * 4
        m0 = at("m0", [HEADS, DEC_B], f32, rw)
        bg = at("bg", [36, 1], f32, rw + 32)
        assert rw + 64 <= hs0 + DV * 4
        late = tmp0
        bhi = at("bhi", [P, KT, TT], f32r, late)
        blo = at("blo", [P, KT, TT], f32r, late + KT * TT * 4)
        hidlo = at("hidlo", [P, HID, TT], f32r, late)
        late += 2 * KT * TT * 4
        yc = at("yc", [P, KT, TT], f32, late)
        late += KT * TT * 4
        sgm = at("sgm", [P, KT, TT], f32, late)
        late += KT * TT * 4
        fr = at("fr", [P, 4, TT], f32, late)
        late += 4 * TT * 4
        sqs = at("sqs", [P, TT], f32, late)
        rst = at("rst", [P, TT], f32, late + TT * 4)
        mu = at("mu", [P, TT], f32, tmp0)
        assert late + 2 * TT * 4 <= 229344

        psum = [ctx.enter_context(nc.psum_tensor(f"product{s}", [P, 2, 512], f32)) for s in range(2)]
        side = ctx.enter_context(nc.psum_tensor("side", [P, 4, 512], f32))

        def tok(ap):
            return ap.rearrange("p (a n) -> p a n", a=2)

        def sem(name):
            return ctx.enter_context(nc.semaphore(name))

        x_in, const_in, gate_in, hist_in = sem("x_in"), sem("const_in"), sem("gate_in"), sem("hist_in")
        raw_in = [sem(f"raw_in{s}") for s in range(2)]
        hb_in, bv_in, x2_in = sem("hb_in"), sem("bv_in"), sem("x2_in")
        c_loaded = [sem(f"c_loaded{s}") for s in range(C_RING)]
        c_saved = [sem(f"c_saved{s}") for s in range(C_RING)]
        rows_out, conv_saved, cst_saved, small_saved, out_saved = (sem(n) for n in (
            "rows_out", "conv_saved", "cst_saved", "small_saved", "out_saved"))
        hi_done, lo_done, chunk_done = sem("hi_done"), sem("lo_done"), sem("chunk_done")
        ready = [sem(f"ready{s}") for s in range(2)]
        drained = [sem(f"drained{s}") for s in range(2)]
        pool_step, dve_step, act_step = sem("pool_step"), sem("dve_step"), sem("act_step")
        sq_ready, sq_added, sum_ready, stat_ready = sem("sq_ready"), sem("sq_added"), sem("sum_ready"), sem("stat_ready")
        ms_ready, root_ready = sem("ms_ready"), sem("root_ready")
        tile_ready, opnd_hi, opnd_lo = sem("tile_ready"), sem("opnd_hi"), sem("opnd_lo")
        gw_hi, gw_lo, gates_ready, fx_ready, ln_ready, rex_ready, rex_done, rows_ready, rowT_ready, rowT_used = (
            sem(n) for n in ("gw_hi", "gw_lo", "gates_ready", "fx_ready", "ln_ready", "rex_ready", "rex_done",
                             "rows_ready", "rowT_ready", "rowT_used"))
        sg_ready, u_done, head_done = sem("sg_ready"), sem("u_done"), sem("head_done")
        kt_ready, kt_used = sem("kt_ready"), sem("kt_used")
        st_ready, w_diag, w_ready, pt_ready = sem("st_ready"), sem("w_diag"), sem("w_ready"), sem("pt_ready")
        expm_ready, wkp_ready, vs_hi, vs_all, kh_ready, ops_ready = (sem(n) for n in (
            "expm_ready", "wkp_ready", "vs_hi", "vs_all", "kh_ready", "ops_ready"))
        den_ready, den_abs, sden_ready, sden_abs = sem("den_ready"), sem("den_abs"), sem("sden_ready"), sem("sden_abs")
        snum_ready, hs_ready, hs_sq, hs_var, hs_std, hs_norm, hst_ready, hst_used = (sem(n) for n in (
            "snum_ready", "hs_ready", "hs_sq", "hs_var", "hs_std", "hs_norm", "hst_ready", "hst_used"))
        hsq_ready, hsum_ready, ss_ready, var_ready, std_ready = (sem(n) for n in (
            "hsq_ready", "hsum_ready", "ss_ready", "var_ready", "std_ready"))
        np_ready, np_used, nn_ready = sem("np_ready"), sem("np_used"), sem("nn_ready")
        conv_ready, mean_ready, xc_ready, cn_ready, csg_ready = (sem(n) for n in (
            "conv_ready", "mean_ready", "xc_ready", "cn_ready", "csg_ready"))
        mem_hi, mem_lo, mixed, x1_ready = sem("mem_hi"), sem("mem_lo"), sem("mixed"), sem("x1_ready")
        hidsq_ready, hid_hi, hid_lo = sem("hidsq_ready"), sem("hid_hi"), sem("hid_lo")
        out_ready = sem("out_ready")
        block = ctx.enter_context(nc.Block())

        def c(name, j):
            return col[:, bass.ds(COLS[name] + j, 1)]

        def tile(buf, j, lo=0, n=TT):
            return buf[:, bass.ds(j, 1), lo:lo + n]

        def wait_filled(eng, h, name):
            s = USES.index(name) % 2
            if name in BY_CHUNK:
                eng.wait_ge(chunk_done, PERHEAD * h + (C_HEAD + BY_CHUNK[name] + 1))
            else:
                eng.wait_ge(ready[s], len(BY_SLOT[s]) * h + (BY_SLOT[s].index(name) + 1))
            return s

        def wait_drained(eng, h, name):
            n = USES.index(name)
            eng.wait_ge(drained[n % 2], USES_HEAD * h + (S_HEAD + n // 2 + 1))

        def apart(eng):
            eng.nop(nofuse=True)

        def halves(ap):
            return ap.rearrange("p a (s n) -> p (a s) n", s=2)

        def slot(s):
            return psum[s][:, :, 0:HALF]

        @block.sync
        def _(sp):
            stream = wstream.rearrange("(n s) p k m -> n s p k m", s=2)
            sp.dma_start(x0[:, :, :], xT).then_inc(x_in, 16)
            sp.dma_start(col[:, :], cols).then_inc(const_in, 16)
            sp.dma_start(wg[:, :, :], w_gates).then_inc(gate_in, 16)
            sp.dma_start(bg[:, :], b_gates).then_inc(gate_in, 16)
            sp.dma_start(m0[:, :], m_in).then_inc(gate_in, 16)
            for s in range(2):
                sp.dma_start(wraw[:, s, :, :], wstream[s, :, :, :]).then_inc(raw_in[s], 16)
            sp.dma_start(wdw[:, :, :], w_dw).then_inc(const_in, 16)
            sp.dma_start(nold[:, :, :, :], n_in).then_inc(const_in, 16)

            def load(first, last):
                with sp.Fori(first, last) as i:
                    for s in range(2):
                        sp.wait_ge(lo_done, 2 * i + (s - 1))
                        sp.dma_start(wraw[:, s, :, :],
                                     stream[bass.ds(i, 1), s, :, :, :].rearrange("a p k m -> p (a k) m")).then_inc(raw_in[s], 16)

            load(1, (C_OUT + 4) // 2)
            sp.wait_ge(mixed, KT)
            sp.dma_start(sgm[:, :, :], xT).then_inc(x2_in, 16)
            load((C_OUT + 4) // 2, N_CHUNKS // 2)
            for j in range(KT):
                sp.wait_ge(out_ready, j + 1)
                sp.dma_start(yT[:, j, :], y[:, j, :]).then_inc(out_saved, 16)
            sp.wait_ge(out_saved, 16 * KT)
            sp.wait_ge(conv_saved, 16 * 2 * KT)
            sp.wait_ge(small_saved, 16 * 4)
            sp.wait_ge(cst_saved, 16 * HEADS)
            for s in range(C_RING):
                sp.wait_ge(c_saved[s], 16 * (DEC_B // C_RING) * HEADS)

        @block.gpsimd
        def _(pool):
            pool.memset(eps[:, :], EPS).then_inc(pool_step, 1)
            pool.memset(ones[:, :], 1.0).then_inc(pool_step, 1)
            pool.memset(ident[:, :], 0.0).then_inc(pool_step, 1)
            pool.memset(causal[:, :], 0.0).then_inc(pool_step, 1)
            pool.memset(causal_s[:, :, :], 0.0).then_inc(pool_step, 1)
            pool.memset(own[:, :], 1.0).then_inc(pool_step, 1)
            pool.memset(u[:, :, 0:HIST], 0.0).then_inc(pool_step, 1)
            pool.memset(qm[:, :, :], 0.0).then_inc(pool_step, 1)
            pool.memset(row["one"][:, :], 1.0).then_inc(pool_step, 1)
            pool.wait_ge(pool_step, 9)
            pool.affine_select(out=ident[:, :], in_=ident[:, :], compare_op=ALU.not_equal, fill=1.0, base=0,
                               pattern=[[-1, P]], channel_multiplier=1).then_inc(pool_step, 1)
            pool.affine_select(out=causal[:, :], in_=causal[:, :], compare_op=ALU.is_ge, fill=-1e30, base=0,
                               pattern=[[1, P]], channel_multiplier=-1).then_inc(pool_step, 1)
            pool.affine_select(out=causal_s[:, :, :], in_=causal_s[:, :, :], compare_op=ALU.is_ge, fill=-1e30, base=0,
                               pattern=[[DEC_T, DEC_B], [1, DEC_T]], channel_multiplier=-1).then_inc(pool_step, 1)
            pool.wait_ge(pool_step, 12)
            pool.affine_select(out=causal_s[:, :, :], in_=causal_s[:, :, :], compare_op=ALU.is_ge, fill=-1e30, base=0,
                               pattern=[[-DEC_T, DEC_B], [0, DEC_T]], channel_multiplier=1).then_inc(pool_step, 1)
            pool.affine_select(out=own[:, :], in_=own[:, :], compare_op=ALU.is_ge, fill=0.0, base=0,
                               pattern=[[-DEC_T, DEC_B]], channel_multiplier=1).then_inc(pool_step, 1)
            pool.wait_ge(pool_step, 14)
            pool.affine_select(out=own[:, :], in_=own[:, :], compare_op=ALU.is_ge, fill=0.0, base=DEC_T - 1,
                               pattern=[[DEC_T, DEC_B]], channel_multiplier=-1).then_inc(pool_step, 1)
            for ct in range(KT):
                dst = u[:, ct, HIST + SEQ:].rearrange("p (b r) -> p b r", r=SROW)[:, :, 0:HIST]
                pool.dma_start(dst, hist[:, ct, :, :]).then_inc(hist_in, 16)
            pool.wait_ge(rows_ready, 1)
            pool.dma_start(rows_dram, rout[:, :]).then_inc(rows_out, 16)
            pool.dma_start(m_p, rout[:, R_M + SEQ - 1:R_M + SEQ]).then_inc(small_saved, 16)
            pool.dma_start(m_s, rout[:, R_M + SEQ:R_M + TT]).then_inc(small_saved, 16)
            pool.wait_ge(rows_out, 16)
            c_in5 = c_in.rearrange("(h b) p k v -> h b p k v", h=HEADS)
            c_s5 = c_s.rearrange("(h b) p k v -> h b p k v", h=HEADS)

            def rows_load(h):
                pool.dma_start(hb[:, :], rows_dram[bass.ds(h, 1), :].broadcast_to([P, N_ROW])).then_inc(hb_in, 16)

            def bias_load(h):
                pool.dma_start(bv[:, :], b_v[bass.ds(h, 1), :].broadcast_to([P, DV])).then_inc(bv_in, 16)

            def state_load(h, b):
                s = b % C_RING
                pool.dma_start(crg[:, s, :, :], c_in5[bass.ds(h, 1), b, :, :, :].rearrange("a p k v -> p (a k) v")).then_inc(c_loaded[s], 16)

            def state_saved(h, b):
                pool.wait_ge(c_saved[b % C_RING], 16 * (DEC_B // C_RING) * h + 16 * (b // C_RING + 1))

            def states(h):
                for b in range(DEC_B):
                    wait_drained(pool, h, f"cu{b}")
                    apart(pool)
                    s = b % C_RING
                    pool.dma_start(c_s5[bass.ds(h, 1), b, :, :, :].rearrange("a p k v -> p (a k) v"), crg[:, s, :, :]).then_inc(c_saved[s], 16)
                    if 1 <= b and b - 1 + C_RING < DEC_B:
                        state_saved(h, b - 1)
                        state_load(h, b - 1 + C_RING)

            def prompt_state(h):
                for name in ("cc01", "cc23"):
                    wait_drained(pool, h, name)
                apart(pool)
                pool.dma_start(c_p[bass.ds(h, 1), :, :, :].rearrange("a v p k -> p (a v) k"), cst[:, :, :]).then_inc(cst_saved, 16)

            rows_load(0)
            bias_load(0)
            for b in range(C_RING):
                state_load(0, b)
            pool.wait_ge(u_done, 2 * KT)
            pool.wait_ge(drained[1], KT)
            pool.wait_ge(hist_in, 16 * KT)
            for ct in range(KT):
                pool.dma_start(conv_p[:, ct, :], u[:, ct, SEQ:SEQ + HIST]).then_inc(conv_saved, 16)
                src = u[:, ct, HIST + SEQ:].rearrange("p (b r) -> p b r", r=SROW)[:, :, DEC_T:SROW]
                pool.dma_start(conv_s[:, ct, :, :], src).then_inc(conv_saved, 16)
            with pool.Fori(0, HEADS - 1) as h:
                states(h)
                rows_load(h + 1)
                for b in range(C_RING):
                    state_saved(h, b + DEC_B - C_RING)
                    state_load(h + 1, b)
                prompt_state(h)
                pool.wait_ge(cst_saved, 16 * h + 16)
                pool.wait_ge(head_done, h + 1)
                bias_load(h + 1)
            states(HEADS - 1)
            prompt_state(HEADS - 1)
            pool.wait_ge(nn_ready, 2 * HEADS)
            pool.dma_start(n_s, nnew[:, :, :, :]).then_inc(small_saved, 16)
            pool.wait_ge(np_used, HEADS)
            pool.dma_start(n_p, npn[:, :, :]).then_inc(small_saved, 16)

        @block.scalar
        def _(act):
            def hi(i, per, k):
                act.wait_ge(raw_in[k % 2], 8 * per * i + 16 * (k // 2 + 1))
                if k >= RING:
                    act.wait_ge(chunk_done, per * i + (k - RING + 1))
                act.activation(whi[:, k % RING, :, :], wraw[:, k % 2, :, :], ACT.Copy).then_inc(hi_done, 1)

            def squares(n, j, src, k):
                if not isinstance(n, int) or n >= 2:
                    act.wait_ge(sq_added, n - 1)
                if not isinstance(n, int):
                    apart(act)
                act.activation(fr[:, k:k + 1, :], src, ACT.Square).then_inc(sq_ready, 1)

            def root(n):
                act.wait_ge(stat_ready, n)
                act.activation(tok(rst[:, :]), side[:, 0:2, 0:HALF], ACT.Ln, bias=eps[:, :], scale=1.0 / D_MODEL).then_inc(ms_ready, 1)
                act.wait_ge(ms_ready, n)
                act.activation(rst[:, :], rst[:, :], ACT.Exp, scale=-0.5).then_inc(root_ready, 1)

            act.wait_ge(x_in, 16)
            for j in range(KT):
                squares(j, j, tile(x0, j), j % 2)
            act.wait_ge(gate_in, 48)
            act.activation(wghi[:, :, :], wg[:, :, :], ACT.Copy).then_inc(gw_hi, 1)
            act.wait_ge(pool_step, 15)
            root(1)
            for j in range(KT):
                act.wait_ge(tile_ready, j + 1)
                act.activation(tile(ahi, j), fr[:, 2 + j % 2:3 + j % 2, :], ACT.Copy).then_inc(opnd_hi, 1)
            for k in range(RING - 1):
                hi(0, 4, k)
            act.wait_ge(fx_ready, 1)
            act.activation(row["ex"][:, :], row["fg"][:, :], ACT.Abs).then_inc(act_step, 1)
            act.wait_ge(act_step, 1)
            act.activation(row["ex"][:, :], row["ex"][:, :], ACT.Exp, scale=-1.0).then_inc(act_step, 1)
            act.wait_ge(act_step, 2)
            act.activation(row["ex"][:, :], row["ex"][:, :], ACT.Ln, bias=1.0).then_inc(ln_ready, 1)
            act.wait_ge(rex_ready, 3)
            act.activation(rout[:, R_WINTER:N_ROW], rout[:, R_WINTER:N_ROW], ACT.Exp).then_inc(rex_done, 1)

            with act.Fori(0, KT // 2) as i:
                for k in range(4):
                    hi(i, 4, k + 3)
                    if k % 2 == 0:
                        j = 2 * i + k // 2
                        act.wait_ge(chunk_done, 4 * i + k + 1)
                        if k > 0:
                            act.wait_ge(drained[1], j)
                        act.activation(halves(sg[:, :].rearrange("p (a t) -> p a t", a=1)), slot(0), ACT.Sigmoid,
                                       bias=c("b_ug", j)).then_inc(drained[0], 1)
                act.wait_ge(drained[1], 2 * i + 2)
                act.wait_ge(chunk_done, 4 * i + 4)

            act.wait_ge(rowT_ready, 1)
            for s in range(ST + 1):
                n = P if s < ST else NS
                act.activation(acol[0:n, s, :], side[0:n, 3, 4 * s:4 * s + 4], ACT.Copy).then_inc(rowT_used, 1)
            act.activation(wkcol[:, :], side[0:NS, 3, 20:24], ACT.Copy).then_inc(rowT_used, 1)
            act.activation(mcol[:, :], side[0:NS, 3, 24:28], ACT.Exp, scale=-1.0).then_inc(rowT_used, 1)
            act.wait_ge(const_in, 48)
            with act.Fori(0, HEADS) as h:
                def use(name):
                    return wait_filled(act, h, name)

                def was_drained(name):
                    wait_drained(act, h, name)

                def split(k):
                    hi(h, PERHEAD, C_HEAD + k)

                split(3)
                split(4)
                act.wait_ge(hb_in, 16 * h + 16)
                act.activation(hb[:, R_M:R_M + SEQ], hb[:, R_M:R_M + SEQ], ACT.Exp, scale=-1.0).then_inc(expm_ready, 1)
                act.wait_ge(rowT_used, ST + 3)
                act.activation(wkp[:, :], acol[:, 0:ST, bass.ds(h, 1)].rearrange("p s a -> p (s a)"), ACT.Exp,
                               bias=hb[:, R_NEGM + SEQ - 1:R_NEGM + SEQ]).then_inc(wkp_ready, 1)
                for s in range(ST - 1):
                    act.activation(pt[:, PT_AT[s] + P:PT_AT[s] + SEQ - P * s], hb[:, R_NEGM + P * (s + 1):R_NEGM + SEQ],
                                   ACT.Exp, bias=acol[:, s, bass.ds(h, 1)]).then_inc(w_ready, 1)
                split(5)
                s = use("k0")
                act.activation(halves(kT[:, 0:1, :]), slot(s), ACT.Identity, bias=c("b_k", 2 * h)).then_inc(drained[s], 1)
                split(6)
                split(7)
                s = use("k1")
                act.activation(halves(kT[:, 1:2, :]), slot(s), ACT.Identity, bias=c("b_k", 2 * h + 1)).then_inc(drained[s], 1)
                act.wait_ge(w_diag, 5 * h + 5)
                apart(act)
                for s in range(ST):
                    d = pt[:, PT_AT[s]:PT_AT[s] + P]
                    act.activation(d, d, ACT.Exp, bias=acol[:, s, bass.ds(h, 1)]).then_inc(w_ready, 1)
                d = pt[0:NS, PT_AT[ST]:N_PT]
                act.activation(d, d, ACT.Exp, bias=acol[0:NS, ST, bass.ds(h, 1)]).then_inc(w_ready, 1)
                was_drained("kts")
                act.activation(kwh[:, :], kws[:, :], ACT.Copy).then_inc(kh_ready, 1)
                act.wait_ge(wkp_ready, h + 1)
                for half in range(2):
                    act.wait_ge(kt_ready, 2 * h + (half + 1))
                    for q in (2 * half, 2 * half + 1):
                        act.activation(kw[:, q, :], side[:, half, DK * (q % 2):DK * (q % 2 + 1)], ACT.Copy,
                                       scale=wkp[:, q:q + 1]).then_inc(kt_used, 1)
                split(8)
                was_drained("v4")
                act.activation(vst[0:NS, :], vtok[0:NS, ST, :], ACT.Copy).then_inc(vs_hi, 1)
                act.activation(vst[64:96, :], vtok[0:NS, ST, :], ACT.Copy).then_inc(vs_all, 1)
                split(9)
                split(10)
                for k in range(VT):
                    split(11 + k)
                    s = use(f"o{k}")
                    act.activation(halves(tile(hm, 4 * h + k)), slot(s), ACT.Sigmoid, bias=c("b_o", 4 * h + k)).then_inc(drained[s], 1)
                    if k == 0:
                        act.wait_ge(den_ready, h + 1)
                        act.activation(rden[:, :], side[:, 0, :], ACT.Abs).then_inc(den_abs, 1)
                        act.wait_ge(sden_ready, h + 1)
                        act.activation(sst[:, 0:1], side[0:NS, 2, 0:1], ACT.Abs).then_inc(sden_abs, 1)
                act.wait_ge(hs_ready, h + 1)
                act.activation(hsq[:, :], hs[:, :], ACT.Square, accum_out=sst[:, 2:3]).then_inc(hs_sq, 1)
                act.wait_ge(hs_sq, h + 1)
                act.activation(sst[:, 3:4], sst[:, 2:3], ACT.Ln, bias=eps[0:NS, :], scale=1.0 / DV).then_inc(hs_var, 1)
                act.wait_ge(hs_var, h + 1)
                act.activation(sst[:, 4:5], sst[:, 3:4], ACT.Exp, scale=-0.5).then_inc(hs_std, 1)
                for k in range(VT):
                    was_drained(f"pv{k}")
                    if k == 3:
                        act.wait_ge(hsum_ready, 3 * h + 1)
                    dst = sqacc[:, :] if k == 0 else sqh[:, k % 2, :]
                    act.activation(dst, hr[:, k % 2, :], ACT.Square).then_inc(hsq_ready, 1)
                act.wait_ge(np_ready, h + 1)
                act.activation(npn[:, bass.ds(h, 1), :], side[:, 2:3, P:P + QT], ACT.Copy).then_inc(np_used, 1)
                for half in range(2):
                    s = use(("cc01", "cc23")[half])
                    act.activation(cst[:, 2 * half:2 * half + 2, :].rearrange("p a k -> p (a k)"), psum[s][:, 0, :],
                                   ACT.Copy).then_inc(drained[s], 1)
                act.wait_ge(ss_ready, h + 1)
                act.activation(sqacc[:, :], side[:, 1, :], ACT.Ln, bias=eps[:, :], scale=1.0 / DV).then_inc(var_ready, 1)
                act.wait_ge(var_ready, h + 1)
                act.activation(sqacc[:, :], sqacc[:, :], ACT.Exp, scale=-0.5).then_inc(std_ready, 1)

            act.wait_ge(head_done, HEADS)
            act.wait_ge(cst_saved, 16 * HEADS)
            for s in range(C_RING):
                act.wait_ge(c_saved[s], 16 * (DEC_B // C_RING) * HEADS)
            with act.Fori(0, KT // 4) as i:
                for k in range(4):
                    hi(i, 4, C_GATE + k + 3)
                    j = 4 * i + k
                    act.wait_ge(chunk_done, 4 * i + (C_GATE + k + 1))
                    act.activation(halves(tile(sgm, j)), slot(k % 2), ACT.Sigmoid, bias=c("b_gm", j)).then_inc(drained[k % 2], 1)
                    act.wait_ge(xc_ready, j + 1)
                    squares(j + KT, j, tile(u, j), k % 2)
            root(2)
            with act.Fori(0, KT // 4) as i:
                for k in range(4):
                    hi(i, 4, C_GATE + KT + k + 3)
                    j = 4 * i + k
                    act.wait_ge(chunk_done, 4 * i + (C_GATE + KT + k + 1))
                    act.activation(halves(tile(yc, j)), slot(k % 2), ACT.Sigmoid, bias=c("b_gc", j)).then_inc(drained[k % 2], 1)
                    act.wait_ge(cn_ready, j + 1)
                    apart(act)
                    act.activation(fr[:, k % 2:k % 2 + 1, :], tile(u, j), ACT.Sigmoid, bias=c("b_cln", j)).then_inc(csg_ready, 1)
                    act.wait_ge(tile_ready, KT + j + 1)
                    apart(act)
                    act.activation(tile(bhi, j), tile(u, j), ACT.Copy).then_inc(opnd_hi, 1)
            with act.Fori(0, KT // 4) as i:
                for k in range(4):
                    hi(i, 4, C_CONV + k + 3)
                    if k == 0:
                        act.wait_ge(chunk_done, C_CONV)
                        apart(act)
                    for q in range(2):
                        act.activation(tile(mhi, 8 * i + 2 * k + q), tile(hm, 8 * i + 2 * k + q), ACT.Copy).then_inc(mem_hi, 1)
            with act.Fori(0, KT // 2) as i:
                for k in range(4):
                    hi(i, 4, C_MEM + k + 3)
                    if k % 2 == 1:
                        j = 2 * i + k // 2
                        act.wait_ge(mixed, j + 1)
                        apart(act)
                        act.activation(tile(bhi, j), tile(yc, j), ACT.Copy).then_inc(opnd_hi, 1)
            with act.Fori(0, KT // 4) as i:
                for k in range(4):
                    hi(i, 4, C_OUT + k + 3)
                    j = 4 * i + k
                    act.wait_ge(chunk_done, 4 * i + (C_OUT + k + 1))
                    act.activation(halves(tile(y, j)), slot(k % 2), ACT.Copy).then_inc(drained[k % 2], 1)
                    act.wait_ge(drained[k % 2], 2 * i + (S_OUT + k // 2 + 1))
                    squares(j + 2 * KT, j, tile(y, j), k % 2)
            root(3)
            for j in range(KT):
                act.wait_ge(x1_ready, j + 1)
                squares(3 * KT + j, j, tile(yc, j), j % 2)
            root(4)
            for j in range(KT):
                act.wait_ge(tile_ready, 2 * KT + j + 1)
                act.activation(tile(ahi, j), fr[:, 2 + j % 2:3 + j % 2, :], ACT.Copy).then_inc(opnd_hi, 1)
            for f in range(2):
                cf = C_FF + PERHALF * f
                sf = S_FF + S_HALF * f
                with act.Fori(0, HID // 4) as i:
                    for k in range(4):
                        hi(i, 4, cf + k + 3)
                        n = HID * f + k + 1
                        act.wait_ge(drained[k % 2], 2 * i + (sf + k // 2 + 1))
                        act.activation(fr[:, 2 + k % 2, :], fr[:, k % 2, :], ACT.Square).then_inc(hidsq_ready, 1)
                        act.wait_ge(hidsq_ready, 4 * i + n)
                        act.activation(tile(hidhi, 4 * i + k), fr[:, 2 + k % 2:3 + k % 2, :], ACT.Copy).then_inc(hid_hi, 1)

                def down(i, ks):
                    for k in range(4):
                        if k in ks:
                            hi(i, 4, cf + HID + k + 3)
                        if k % 2 == 1:
                            j = 2 * i + k // 2
                            if f == 0:
                                act.wait_ge(chunk_done, 4 * i + (cf + HID + k + 1))
                                act.activation(halves(tile(sgm, j)), slot(k // 2), ACT.Identity, bias=c("b_ff2", j)).then_inc(drained[k // 2], 1)
                            else:
                                act.wait_ge(drained[k // 2], i + (sf + HID // 2 + 1))
                                squares(4 * KT + j, j, tile(y, j), k // 2)

                turns = KT // 2 - f
                with act.Fori(0, turns) as i:
                    down(i, range(4))
                if f == 1:
                    down(turns, range(1))
            root(5)

        @block.vector
        def _(dve):
            V = nc.vector
            st = Steps()

            def mark(ins):
                ins.then_inc(dve_step, 1)
                return st.add()

            def lo(i, per, k):
                dve.wait_ge(hi_done, per * i + (k + 1))
                V.tensor_tensor(wlo[:, k % RING, :, :], wraw[:, k % 2, :, :], whi[:, k % RING, :, :].bitcast(f32),
                                ALU.subtract).then_inc(lo_done, 1)

            def add_square(n, k, base=None):
                dve.wait_ge(sq_ready, n + 1)
                if base is None:
                    dve.wait_ge(sq_added, n)
                V.tensor_tensor(sqs[:, :], sqs[:, :], fr[:, k, :], ALU.add).then_inc(sq_added, 1)

            rst3 = rst[:, :].rearrange("p (a t) -> p a t", a=1)

            dve.wait_ge(dve_step, mark(V.memset(sqs[:, :], 0.0)))
            for j in range(KT):
                add_square(j, j % 2)
            dve.wait_ge(gw_hi, 1)
            V.tensor_tensor(wglo[:, :, :], wg[:, :, :], wghi[:, :, :].bitcast(f32), ALU.subtract).then_inc(gw_lo, 1)
            dve.wait_ge(root_ready, 1)
            dve.wait_ge(const_in, 48)
            for j in range(KT):
                V.scalar_tensor_tensor(fr[:, 2 + j % 2:3 + j % 2, :], tile(x0, j), c("g_pre_mix", j), rst3, ALU.mult,
                                       ALU.mult).then_inc(tile_ready, 1)
                dve.wait_ge(opnd_hi, j + 1)
                V.tensor_tensor(tile(alo, j), fr[:, 2 + j % 2:3 + j % 2, :], tile(ahi, j).bitcast(f32), ALU.subtract).then_inc(opnd_lo, 1)
            for k in range(RING - 1):
                lo(0, 4, k)
            dve.wait_ge(gates_ready, 1)
            dve.wait_ge(gate_in, 48)
            dve.wait_ge(pool_step, 15)
            r2 = lambda name: row[name][:, :].rearrange("p (a n) -> p a n", a=2)
            V.tensor_scalar(r2("fg"), side[32:36, 0:2, 0:HALF], bg[32:36, :], None, ALU.add).then_inc(fx_ready, 1)
            ig = mark(V.tensor_scalar(r2("ig"), side[0:4, 0:2, 0:HALF], bg[0:4, :], None, ALU.add))
            dve.wait_ge(ln_ready, 1)
            lf = mark(V.scalar_tensor_tensor(row["fg"][:, :], row["fg"][:, :], 0.0, row["ex"][:, :], ALU.min, ALU.subtract))
            dve.wait_ge(dve_step, lf)
            mark(V.tensor_tensor_scan(row["B"][:, 0:SEQ], row["one"][:, 0:SEQ], row["fg"][:, 0:SEQ], 0.0, ALU.mult, ALU.add))
            seq = lambda name: row[name][:, SEQ:TT].rearrange("h (b t) -> h b t", t=DEC_T)
            n = mark(V.tensor_copy(seq("B")[:, :, 0], seq("fg")[:, :, 0]))
            for t in range(1, DEC_T):
                dve.wait_ge(dve_step, n)
                n = mark(V.tensor_tensor(seq("B")[:, :, t], seq("B")[:, :, t - 1], seq("fg")[:, :, t], ALU.add))
            dve.wait_ge(dve_step, n)
            n = mark(V.tensor_tensor(row["a"][:, :], row["ig"][:, :], row["B"][:, :], ALU.subtract))
            dve.wait_ge(dve_step, n)
            mark(V.tensor_tensor_scan(row["M"][:, 0:SEQ], row["a"][:, 0:SEQ], row["a"][:, 0:SEQ], 0.0, ALU.max, ALU.max))
            n = mark(V.tensor_tensor(seq("M")[:, :, 0], seq("a")[:, :, 0], m0[:, :], ALU.max))
            for t in range(1, DEC_T):
                dve.wait_ge(dve_step, n)
                n = mark(V.tensor_tensor(seq("M")[:, :, t], seq("M")[:, :, t - 1], seq("a")[:, :, t], ALU.max))
            dve.wait_ge(dve_step, n)
            mark(V.tensor_tensor(rout[:, R_M:R_M + TT], row["B"][:, :], row["M"][:, :], ALU.add))
            mark(V.tensor_scalar(rout[:, R_NEGM:R_NEGM + TT], row["M"][:, :], -1.0, None, ALU.mult))
            last = seq("M")[:, :, DEC_T - 1]
            V.tensor_tensor(rout[:, R_WINTER:R_WK].rearrange("h (b t) -> h b t", t=DEC_T),
                            m0[:, :].rearrange("h (b a) -> h b a", a=1).broadcast_to([HEADS, DEC_B, DEC_T]), seq("M"),
                            ALU.subtract).then_inc(rex_ready, 1)
            V.tensor_tensor(rout[:, R_WK:R_DEC].rearrange("h (b t) -> h b t", t=DEC_T), seq("a"),
                            seq("M")[:, :, DEC_T - 1:DEC_T].broadcast_to([HEADS, DEC_B, DEC_T]), ALU.subtract).then_inc(rex_ready, 1)
            V.tensor_tensor(rout[:, R_DEC:N_ROW], m0[:, :], last, ALU.subtract).then_inc(rex_ready, 1)
            dve.wait_ge(rex_done, 1)
            dve.wait_ge(dve_step, st.n)
            V.tensor_copy(row["one"][:, 0:4], row["one"][:, 4:8]).then_inc(rows_ready, 1)

            with dve.Fori(0, KT // 2) as i:
                for k in range(4):
                    lo(i, 4, k + 3)
                    if k % 2 == 1:
                        j = 2 * i + k // 2
                        dve.wait_ge(chunk_done, 4 * i + k + 1)
                        dve.wait_ge(drained[0], j + 1)
                        V.scalar_tensor_tensor(tile(u, j, HIST, HALF), psum[1][:, 0:1, 0:HALF], c("b_ua", j),
                                               sg[:, 0:HALF].rearrange("p (a t) -> p a t", a=1), ALU.add, ALU.mult).then_inc(u_done, 1)
                        V.scalar_tensor_tensor(tile(u, j, HIST + HALF, SEQ - HALF), psum[1][:, 1:2, 0:SEQ - HALF], c("b_ua", j),
                                               sg[:, HALF:SEQ].rearrange("p (a t) -> p a t", a=1), ALU.add, ALU.mult).then_inc(u_done, 1)
                        new = tile(u, j, HIST + SEQ, DEC_B * SROW).rearrange("p a (b r) -> p (a b) r", r=SROW)[:, :, HIST:SROW]
                        V.scalar_tensor_tensor(new, psum[1][:, 1, SEQ - HALF:HALF].rearrange("p (b t) -> p b t", t=DEC_T),
                                               c("b_ua", j), sg[:, SEQ:TT].rearrange("p (b t) -> p b t", t=DEC_T),
                                               ALU.add, ALU.mult).then_inc(drained[1], 1)

            dve.wait_ge(hist_in, 16 * KT)
            dve.wait_ge(rowT_used, ST + 3)
            dve.wait_ge(rows_out, 16)
            dve.wait_ge(small_saved, 32)
            dve.wait_ge(u_done, 2 * KT)
            dve.wait_ge(drained[1], KT)
            with dve.Fori(0, HEADS) as h:
                st.loop(h, DVE_PER_HEAD)
                own3 = own[:, :].rearrange("s (b a) -> s b a", a=1).broadcast_to([NS, DEC_B, DK])
                hh = bass.ds(h, 1)

                def use(name):
                    return wait_filled(dve, h, name)

                def was_drained(name):
                    wait_drained(dve, h, name)

                def split(k):
                    lo(h, PERHEAD, C_HEAD + k)

                def taps(first, last):
                    for tap in range(first, last):
                        if tap > 0:
                            dve.wait_ge(dve_step, conv_at[0])
                        for q in range(2):
                            w = wdw[:, bass.ds(2 * h + q, 1), tap].rearrange("p a -> p (a)")
                            src = tile(u, 2 * h + q, tap, SEQ)
                            ssrc = tile(u, 2 * h + q, HIST + SEQ, DEC_B * SROW).rearrange("p a (b r) -> p (a b) r", r=SROW)[:, :, tap:tap + DEC_T]
                            ap, sp_ = accp[:, q:q + 1, :], accs[:, q, :].rearrange("p (b t) -> p b t", t=DEC_T)
                            if tap == 0:
                                mark(V.tensor_scalar(ap, src, w, c("b_dw", 2 * h + q), ALU.mult, ALU.add))
                                mark(V.tensor_scalar(sp_, ssrc, w, c("b_dw", 2 * h + q), ALU.mult, ALU.add))
                            else:
                                mark(V.scalar_tensor_tensor(ap, src, w, ap, ALU.mult, ALU.add))
                                mark(V.scalar_tensor_tensor(sp_, ssrc, w, sp_, ALU.mult, ALU.add))
                        conv_at[0] = st.off + st.n

                conv_at = [0]
                split(3)
                s = use("q0")
                V.tensor_scalar(halves(qT[:, 0:1, :]), slot(s), c("b_q", 2 * h), DK ** -0.5, ALU.add, ALU.mult).then_inc(drained[s], 1)
                taps(0, 2)
                split(4)
                s = use("q1")
                V.tensor_scalar(halves(qT[:, 1:2, :]), slot(s), c("b_q", 2 * h + 1), DK ** -0.5, ALU.add, ALU.mult).then_inc(drained[s], 1)
                dve.wait_ge(hb_in, 16 * h + 16)
                for s in range(ST):
                    V.tensor_tensor(pt[:, PT_AT[s]:PT_AT[s] + P], hb[:, R_NEGM + P * s:R_NEGM + P * (s + 1)], causal[:, :],
                                    ALU.add).then_inc(w_diag, 1)
                V.tensor_tensor(pt[0:NS, PT_AT[ST]:N_PT], hb[0:NS, R_NEGM + SEQ:R_NEGM + TT],
                                causal_s[:, :, :].rearrange("s b t -> s (b t)"), ALU.add).then_inc(w_diag, 1)
                was_drained("q0")
                was_drained("q1")
                qd = [qm[:, kk, :].rearrange("p (b c) -> p b c", c=36)[:, :, 0:DEC_T] for kk in range(QT)]
                for kk in range(QT):
                    V.tensor_tensor(qd[kk], qT[:, kk, SEQ:TT].rearrange("p (b t) -> p b t", t=DEC_T),
                                    hb[:, R_WINTER:R_WK].rearrange("p (b t) -> p b t", t=DEC_T), ALU.mult).then_inc(ops_ready, 1)
                split(5)
                dve.wait_ge(ops_ready, 8 * h + 2)
                for kk in range(QT):
                    V.tensor_tensor(qn[:, kk, :].rearrange("p (b t) -> p b t", t=DEC_T), qd[kk],
                                    nold[:, hh, kk, :].rearrange("p a (b c) -> p (a b) c", c=1).broadcast_to([P, DEC_B, DEC_T]),
                                    ALU.mult).then_inc(ops_ready, 1)
                split(6)
                taps(2, 4)
                split(7)
                was_drained("k1")
                n = 0
                for kk in range(QT):
                    n = mark(V.tensor_tensor(kn[:, kk, :], kT[:, kk, SEQ:TT], hb[:, R_WK:R_DEC], ALU.mult))
                for kk in range(QT):
                    n = mark(V.tensor_tensor(nd[:, kk, :], nold[:, hh, kk, :].rearrange("p a b -> p (a b)"), hb[:, R_DEC:N_ROW], ALU.mult))
                dve.wait_ge(dve_step, n)
                for kk in range(QT):
                    n = mark(V.tensor_reduce(kr[:, kk, :], kn[:, kk, :].rearrange("p (b t) -> p b t", t=DEC_T), X, ALU.add))
                dve.wait_ge(dve_step, n)
                for kk in range(QT):
                    V.tensor_tensor(nnew[:, hh, kk, :].rearrange("p a b -> p (a b)"), nd[:, kk, :], kr[:, kk, :], ALU.add).then_inc(nn_ready, 1)
                dve.wait_ge(bv_in, 16 * h + 16)
                for s_ in range(ST + 1):
                    s = use(f"v{s_}")
                    n_ = P if s_ < ST else NS
                    V.tensor_tensor(vtok[0:n_, s_, :], psum[s][0:n_, 0, :], bv[0:n_, :], ALU.add).then_inc(drained[s], 1)
                    if s_ == 0:
                        s = use("kts")
                        V.tensor_scalar(kws[:, :], psum[s][0:NS, 0, 0:DK], wkcol[:, hh], None, ALU.mult).then_inc(drained[s], 1)
                        dve.wait_ge(kh_ready, h + 1)
                        n = mark(V.tensor_tensor(kwl[:, :], kws[:, :], kwh[:, :].bitcast(f32), ALU.subtract))
                    if s_ < 3:
                        if s_ == 2:
                            dve.wait_ge(dve_step, n)
                            apart(dve)
                        src = (kwl[:, :] if s_ == 2 else kwh[:, :].bitcast(f32)).rearrange("s (a k) -> s a k", a=1)
                        V.tensor_tensor(kst[NS * s_:NS * (s_ + 1), :, :], src.broadcast_to([NS, DEC_B, DK]), own3, ALU.mult).then_inc(ops_ready, 1)
                    if s_ < ST:
                        taps(*V_TAPS[s_])
                split(8)
                dve.wait_ge(vs_hi, h + 1)
                V.tensor_tensor(vst[NS:2 * NS, :], vtok[0:NS, ST, :], vst[0:NS, :].bitcast(f32), ALU.subtract).then_inc(ops_ready, 1)
                dve.wait_ge(st_ready, 5 * h + 5)
                for s in range(ST + 1):
                    dve.wait_ge(w_ready, 8 * h + ST + s)
                    bank, at_ = ST_AT[s]
                    n_, w_ = (P, SEQ - P * s) if s < ST else (NS, NS)
                    d = pt[0:n_, PT_AT[s]:PT_AT[s] + w_]
                    V.tensor_tensor(d, d, side[0:n_, bank, at_:at_ + w_], ALU.mult).then_inc(pt_ready, 1)
                split(9)
                split(10)
                for k in range(VT):
                    split(11 + k)
                    if k == 0:
                        dve.wait_ge(den_abs, h + 1)
                        dve.wait_ge(expm_ready, h + 1)
                        n = mark(V.tensor_tensor(rden[:, :], rden[:, :], hb[:, R_M:R_M + SEQ], ALU.max))
                        dve.wait_ge(sden_abs, h + 1)
                        n2 = mark(V.tensor_tensor(sst[:, 0:1], sst[:, 0:1], mcol[:, hh], ALU.max))
                    for b in (2 * k, 2 * k + 1):
                        s = use(f"cu{b}")
                        V.scalar_tensor_tensor(crg[:, b % C_RING, :, :], crg[:, b % C_RING, :, :], hb[:, R_DEC + b:R_DEC + b + 1],
                                               psum[s][:, :, :], ALU.mult, ALU.add).then_inc(drained[s], 1)
                        if b == 1:
                            dve.wait_ge(dve_step, n2)
                            n = mark(V.reciprocal(rden[:, :], rden[:, :]))
                            n2 = mark(V.reciprocal(sst[:, 1:2], sst[:, 0:1]))
                        else:
                            taps(*C_TAPS[b])
                dve.wait_ge(snum_ready, h + 1)
                dve.wait_ge(dve_step, n2)
                V.tensor_scalar(hs[:, :], side[0:NS, 3, :], sst[:, 1:2], None, ALU.mult).then_inc(hs_ready, 1)
                dve.wait_ge(dve_step, n)
                for k in range(VT):
                    s = use(f"pv{k}")
                    if k >= 2:
                        dve.wait_ge(hsq_ready, VT * h + (k - 1))
                    V.tensor_tensor(hr[:, k % 2, :], psum[s][:, 0, :], rden[:, :], ALU.mult).then_inc(drained[s], 1)
                    if k == 2:
                        dve.wait_ge(hs_std, h + 1)
                        V.tensor_scalar(hs[:, :], hs[:, :], sst[:, 4:5], None, ALU.mult).then_inc(hs_norm, 1)
                    was_drained(f"pv{k}")
                    d = tile(hm, 4 * h + k, 0, SEQ)
                    n = mark(V.tensor_tensor(d, d, hr[:, k % 2:k % 2 + 1, :], ALU.mult))
                    if k >= 1:
                        dve.wait_ge(hsq_ready, VT * h + (k + 1))
                        if k >= 2:
                            dve.wait_ge(hsum_ready, 3 * h + (k - 1))
                        V.tensor_tensor(sqacc[:, :], sqacc[:, :], sqh[:, k % 2, :], ALU.add).then_inc(hsum_ready, 1)
                taps(27, 31)
                dve.wait_ge(conv_saved, 16 * 2 * KT)
                dve.wait_ge(dve_step, conv_at[0])
                apart(dve)
                for q in range(2):
                    mark(V.tensor_copy(tile(u, 2 * h + q, 0, SEQ), accp[:, q:q + 1, :]))
                    m = mark(V.tensor_copy(tile(u, 2 * h + q, SEQ, NS), accs[:, q:q + 1, :]))
                dve.wait_ge(hst_ready, h + 1)
                for k in range(VT):
                    d = tile(hm, 4 * h + k, SEQ, NS)
                    V.scalar_tensor_tensor(d, side[:, 3:4, NS * k:NS * (k + 1)], c("g_mh", 4 * h + k), d, ALU.mult,
                                           ALU.mult).then_inc(hst_used, 1)
                dve.wait_ge(std_ready, h + 1)
                dve.wait_ge(dve_step, m)
                apart(dve)
                for k in range(VT):
                    d = tile(hm, 4 * h + k, 0, SEQ)
                    ins = V.scalar_tensor_tensor(d, d, c("g_mh", 4 * h + k), sqacc[:, :].rearrange("p (a t) -> p a t", a=1), ALU.mult, ALU.mult)
                    if k < VT - 1:
                        mark(ins)
                    else:
                        ins.then_inc(head_done, 1)
            st.leave(HEADS)

            dve.wait_ge(head_done, HEADS)
            dve.wait_ge(cst_saved, 16 * HEADS)
            for s in range(C_RING):
                dve.wait_ge(c_saved[s], 16 * (DEC_B // C_RING) * HEADS)
            dve.wait_ge(dve_step, st.n)
            V.memset(sqs[:, :], 0.0).then_inc(conv_ready, 1)
            dve.wait_ge(mean_ready, 1)
            n = mark(V.tensor_scalar(mu[:, :].rearrange("p (a n) -> p a n", a=2), side[:, 2:4, 0:HALF], 1.0 / D_MODEL, None, ALU.mult))
            dve.wait_ge(dve_step, n)
            dve.wait_ge(conv_ready, 1)
            with dve.Fori(0, KT // 4) as i:
                for k in range(4):
                    lo(i, 4, C_GATE + k + 3)
                    j = 4 * i + k
                    V.tensor_tensor(tile(u, j, 0, TT), tile(u, j, 0, TT), mu[:, :].rearrange("p (a t) -> p a t", a=1),
                                    ALU.subtract).then_inc(xc_ready, 1)
                    add_square(KT + j, k % 2)
            dve.wait_ge(root_ready, 2)
            with dve.Fori(0, KT // 4) as i:
                for k in range(4):
                    lo(i, 4, C_GATE + KT + k + 3)
                    j = 4 * i + k
                    V.scalar_tensor_tensor(tile(u, j), tile(u, j), c("g_cln", j), rst3, ALU.mult, ALU.mult).then_inc(cn_ready, 1)
                    dve.wait_ge(csg_ready, j + 1)
                    V.scalar_tensor_tensor(tile(u, j), tile(u, j), c("b_cln", j), fr[:, k % 2:k % 2 + 1, :], ALU.add, ALU.mult).then_inc(tile_ready, 1)
                    dve.wait_ge(opnd_hi, KT + j + 1)
                    V.tensor_tensor(tile(blo, j), tile(u, j), tile(bhi, j).bitcast(f32), ALU.subtract).then_inc(opnd_lo, 1)
            with dve.Fori(0, KT // 4) as i:
                for k in range(4):
                    lo(i, 4, C_CONV + k + 3)
                    j = 4 * i + k
                    for q in range(2):
                        m = 8 * i + 2 * k + q
                        dve.wait_ge(mem_hi, m + 1)
                        V.tensor_tensor(tile(mlo, m), tile(hm, m), tile(mhi, m).bitcast(f32), ALU.subtract).then_inc(mem_lo, 1)
                    dve.wait_ge(chunk_done, 4 * i + (C_CONV + k + 1))
                    V.tensor_tensor(halves(tile(yc, j)), slot(k % 2), halves(tile(yc, j)), ALU.mult).then_inc(drained[k % 2], 1)
            with dve.Fori(0, KT // 2) as i:
                for k in range(4):
                    lo(i, 4, C_MEM + k + 3)
                    if k % 2 == 1:
                        s, j = k // 2, 2 * i + k // 2
                        dve.wait_ge(chunk_done, 4 * i + (C_MEM + k + 1))
                        V.tensor_tensor(halves(fr[:, s:s + 1, :]), slot(s), halves(tile(sgm, j)), ALU.mult).then_inc(drained[s], 1)
                        dve.wait_ge(drained[s], i + (S_MEM + 1))
                        V.tensor_tensor(tile(yc, j), tile(yc, j), fr[:, s:s + 1, :], ALU.add).then_inc(mixed, 1)
                        dve.wait_ge(opnd_hi, 2 * KT + j + 1)
                        V.tensor_tensor(tile(blo, j), tile(yc, j), tile(bhi, j).bitcast(f32), ALU.subtract).then_inc(opnd_lo, 1)
            dve.wait_ge(sq_added, 2 * KT)
            n = mark(V.memset(sqs[:, :], 0.0))
            dve.wait_ge(dve_step, n)
            with dve.Fori(0, KT // 4) as i:
                for k in range(4):
                    lo(i, 4, C_OUT + k + 3)
                    dve.wait_ge(sq_ready, 4 * i + (2 * KT + k + 1))
                    dve.wait_ge(sq_added, 4 * i + (2 * KT + k))
                    V.tensor_tensor(sqs[:, :], sqs[:, :], fr[:, k % 2, :], ALU.add).then_inc(sq_added, 1)
            dve.wait_ge(root_ready, 3)
            n = mark(V.memset(sqs[:, :], 0.0))
            dve.wait_ge(dve_step, n)
            dve.wait_ge(x2_in, 16)
            for j in range(KT):
                n = mark(V.scalar_tensor_tensor(tile(y, j), tile(y, j), c("g_post_mix", j), rst3, ALU.mult, ALU.mult))
                dve.wait_ge(dve_step, n)
                V.tensor_tensor(tile(yc, j), tile(y, j), tile(sgm, j), ALU.add).then_inc(x1_ready, 1)
                if j >= 1:
                    add_square(3 * KT + j - 1, (j - 1) % 2)
            add_square(4 * KT - 1, 1)
            dve.wait_ge(root_ready, 4)
            dve.wait_ge(x1_ready, KT)
            for j in range(KT):
                V.scalar_tensor_tensor(fr[:, 2 + j % 2:3 + j % 2, :], tile(yc, j), c("g_pre_ff", j), rst3, ALU.mult,
                                       ALU.mult).then_inc(tile_ready, 1)
                dve.wait_ge(opnd_hi, 3 * KT + j + 1)
                V.tensor_tensor(tile(alo, j), fr[:, 2 + j % 2:3 + j % 2, :], tile(ahi, j).bitcast(f32), ALU.subtract).then_inc(opnd_lo, 1)
            n = mark(V.memset(sqs[:, :], 0.0))
            dve.wait_ge(dve_step, n)
            for f in range(2):
                cf = C_FF + PERHALF * f
                sf = S_FF + S_HALF * f
                with dve.Fori(0, HID // 4) as i:
                    for k in range(4):
                        lo(i, 4, cf + k + 3)
                        n = HID * f + k + 1
                        dve.wait_ge(chunk_done, 4 * i + (cf + k + 1))
                        V.tensor_scalar(halves(fr[:, k % 2:k % 2 + 1, :]), slot(k % 2), c("b_ff1", 4 * i + (HID * f + k)), 0.0,
                                        ALU.add, ALU.max).then_inc(drained[k % 2], 1)
                        dve.wait_ge(hid_hi, 4 * i + n)
                        V.tensor_tensor(tile(hidlo, 4 * i + k), fr[:, 2 + k % 2:3 + k % 2, :], tile(hidhi, 4 * i + k).bitcast(f32),
                                        ALU.subtract).then_inc(hid_lo, 1)

                def down(i, ks):
                    for k in range(4):
                        if k in ks:
                            lo(i, 4, cf + HID + k + 3)
                        if k % 2 == 1 and f == 1:
                            s, j = k // 2, 2 * i + k // 2
                            dve.wait_ge(chunk_done, 4 * i + (cf + HID + k + 1))
                            V.tensor_tensor(halves(tile(y, j)), slot(s), halves(tile(sgm, j)), ALU.add).then_inc(drained[s], 1)
                            dve.wait_ge(sq_ready, j + (4 * KT + 1))
                            dve.wait_ge(sq_added, j + 4 * KT)
                            V.tensor_tensor(sqs[:, :], sqs[:, :], fr[:, s, :], ALU.add).then_inc(sq_added, 1)

                turns = KT // 2 - f
                with dve.Fori(0, turns) as i:
                    down(i, range(4))
                if f == 1:
                    down(turns, range(1))
            dve.wait_ge(root_ready, 5)
            for j in range(KT):
                n = mark(V.scalar_tensor_tensor(tile(y, j), tile(y, j), c("g_post_ff", j), rst3, ALU.mult, ALU.mult))
                dve.wait_ge(dve_step, n)
                V.tensor_tensor(tile(y, j), tile(y, j), tile(yc, j), ALU.add).then_inc(out_ready, 1)

        @block.tensor
        def _(pe):
            def mm(out, lhsT, rhs, start, stop, check=False):
                return pe.matmul(out, lhsT, rhs, start=start, stop=stop, skip_group_check=check)

            def product(s, w, xhi, xlo, first=True, last=True, x_at=0):
                n = 0
                for kt in range(KT):
                    for a, b in ((whi, xhi), (whi, xlo), (wlo, xhi)):
                        for g in range(2):
                            ins = mm(psum[s][:, g, 0:HALF], a[:, w, kt, :], b[:, x_at + kt, HALF * g:HALF * (g + 1)],
                                     first and n == 0, last and n == 3 * KT - 1)
                        n += 1
                return ins

            def ring(i, per, k):
                pe.wait_ge(lo_done, per * i + (k + 1))
                return k % RING

            def free(s, n):
                pe.wait_ge(drained[s], n)

            def column_sums(src, banks):
                for g in range(2):
                    ins = mm(side[:, banks + g, 0:HALF], ones[:, :], src[:, HALF * g:HALF * (g + 1)], True, True)
                return ins

            pe.wait_ge(pool_step, 15)
            pe.wait_ge(const_in, 48)
            pe.wait_ge(sq_added, KT)
            column_sums(sqs, 0).then_inc(stat_ready, 1)
            pe.wait_ge(gw_lo, 1)
            pe.wait_ge(opnd_lo, KT)
            n = 0
            for kt in range(KT):
                for a, b in ((wghi, ahi), (wghi, alo), (wglo, ahi)):
                    for g in range(2):
                        ins = mm(side[0:36, g, 0:HALF], a[:, kt, :], b[:, kt, HALF * g:HALF * (g + 1)], n == 0, n == 3 * KT - 1)
                    n += 1
            ins.then_inc(gates_ready, 1)

            def glu(i, k):
                s, j = k % 2, 2 * i + k // 2
                w = ring(i, 4, k)
                if not isinstance(i, int) or j > 0:
                    free(s, j)
                product(s, w, ahi, alo).then_inc(chunk_done, 1)

            for k in range(4):
                glu(0, k)
            with pe.Fori(1, KT // 2) as i:
                for k in range(4):
                    glu(i, k)
            pe.wait_ge(rows_ready, 1)
            for s in range(ST + 1):
                n_ = P if s < ST else NS
                pe.transpose(side[0:n_, 3, 4 * s:4 * s + 4], row["a"][:, P * s:P * s + n_], ident[0:4, 0:4])
            pe.transpose(side[0:NS, 3, 20:24], rout[:, R_WK:R_DEC], ident[0:4, 0:4])
            pe.transpose(side[0:NS, 3, 24:28], rout[:, R_M + SEQ:R_M + TT], ident[0:4, 0:4]).then_inc(rowT_ready, 1)

            with pe.Fori(0, HEADS) as h:
                def use(name):
                    n = USES.index(name)
                    free(n % 2, USES_HEAD * h + (S_HEAD + n // 2))
                    return n % 2

                def was_drained(name):
                    wait_drained(pe, h, name)

                def chunk(name, k):
                    w = ring(h, PERHEAD, C_HEAD + k)
                    s = use(name)
                    product(s, w, ahi, alo).then_inc(chunk_done, 1)

                for k, name in enumerate(("q0", "q1", "k0", "k1")):
                    chunk(name, k)
                def values(q, chunks):
                    s = USES.index(f"v{q}") % 2
                    n_ = P if q < ST else NS
                    n = 0
                    for kt in range(KT):
                        for a, b in ((whi, ahi), (whi, alo), (wlo, ahi)):
                            ins = mm(psum[s][0:n_, 0, P * chunks.start:P * chunks.stop].rearrange("p (c m) -> p c m", m=P),
                                     b[:, kt, P * q:P * q + n_], a[:, chunks.start:chunks.stop, kt, :], n == 0, n == 3 * KT - 1)
                            n += 1
                    return ins

                s = use("v0")
                for part in (range(0, 2), range(2, 4)):
                    for k in part:
                        ring(h, PERHEAD, C_HEAD + 4 + k)
                    ins = values(0, part)
                ins.then_inc(ready[s], 1)
                was_drained("k1")
                s = use("kts")
                for kk in range(QT):
                    ins = pe.transpose(psum[s][0:NS, 0, P * kk:P * (kk + 1)], kT[:, kk, SEQ:TT], ident[:, :])
                ins.then_inc(ready[s], 1)
                was_drained("q0")
                was_drained("q1")
                apart(pe)
                for half in range(2):
                    for q in range(2):
                        for kk in range(QT):
                            t = P * (2 * half + q)
                            ins = pe.transpose(side[:, half, DK * q + P * kk:DK * q + P * (kk + 1)], kT[:, kk, t:t + P], ident[:, :])
                    ins.then_inc(kt_ready, 1)
                for q in range(1, ST + 1):
                    s = use(f"v{q}")
                    ins = values(q, range(4))
                    if q < ST:
                        ins.then_inc(ready[s], 1)
                    else:
                        ins.then_inc(chunk_done, 4)
                pe.wait_ge(kt_used, ST * h + ST)
                apart(pe)
                for q in range(ST + 1):
                    bank, at_ = ST_AT[q]
                    n_, w_ = (P, SEQ - P * q) if q < ST else (NS, NS)
                    for kk in range(QT):
                        ins = mm(side[0:n_, bank, at_:at_ + w_], kT[:, kk, P * q:P * q + n_], qT[:, kk, P * q:P * q + w_],
                                 kk == 0, kk == QT - 1)
                    ins.then_inc(st_ready, 1)
                for k in range(VT):
                    chunk(f"o{k}", 8 + k)
                    if k == 0:
                        pe.wait_ge(pt_ready, 5 * h + 5)
                        pe.wait_ge(ops_ready, 8 * h + 8)
                        for q in range(ST):
                            ins = mm(side[:, 0, P * q:SEQ], ones[:, :], pt[:, PT_AT[q]:PT_AT[q] + SEQ - P * q], q == 0, q == ST - 1)
                        ins.then_inc(den_ready, 1)
                        mm(side[0:NS, 2, 0:1], pt[0:NS, PT_AT[ST]:N_PT], ones[0:NS, 0:1], True, False)
                        for kk in range(QT):
                            ins = mm(side[0:NS, 2, 0:1], qn[:, kk, :], ones[:, 0:1], False, kk == QT - 1)
                        ins.then_inc(sden_ready, 1)
                        mm(side[0:NS, 3, :], pt[0:NS, PT_AT[ST]:N_PT], vtok[0:NS, ST, :], True, False)
                    pe.wait_ge(vs_all, h + 1)
                    for b in (2 * k, 2 * k + 1):
                        pe.wait_ge(c_loaded[b % C_RING], 16 * (DEC_B // C_RING) * h + 16 * (b // C_RING + 1))
                        for kk in range(QT):
                            ins = mm(side[0:NS, 3, :], qm[:, kk, NS * b:NS * (b + 1)], crg[:, b % C_RING, kk, :], False,
                                     b == DEC_B - 1 and kk == QT - 1)
                        if b == DEC_B - 1:
                            ins.then_inc(snum_ready, 1)
                        s = use(f"cu{b}")
                        for kk in range(QT):
                            ins = mm(psum[s][:, kk, :], kst[:, b, P * kk:P * (kk + 1)], vst[:, :], True, True)
                        ins.then_inc(ready[s], 1)
                for k in range(VT):
                    s = use(f"pv{k}")
                    for q in range(ST):
                        ins = mm(psum[s][:, 0, P * q:SEQ], vtok[:, q, P * k:P * (k + 1)], pt[:, PT_AT[q]:PT_AT[q] + SEQ - P * q],
                                 q == 0, q == ST - 1)
                    ins.then_inc(ready[s], 1)
                pe.wait_ge(sden_abs, h + 1)
                for kk in range(QT):
                    for q in range(ST):
                        ins = mm(side[:, 2, P + kk:P + kk + 1], kw[:, q, P * kk:P * (kk + 1)], ones[:, 0:1], q == 0, q == ST - 1)
                ins.then_inc(np_ready, 1)
                for half in range(2):
                    s = use(("cc01", "cc23")[half])
                    for r in range(2):
                        for q in range(ST):
                            v = P * (2 * half + r)
                            ins = mm(psum[s][:, 0, DK * r:DK * (r + 1)], vtok[:, q, v:v + P], kw[:, q, :], q == 0, q == ST - 1)
                    ins.then_inc(ready[s], 1)
                pe.wait_ge(hsum_ready, 3 * h + 3)
                mm(side[:, 1, :], ones[:, :], sqacc[:, :], True, True).then_inc(ss_ready, 1)
                pe.wait_ge(hs_norm, h + 1)
                apart(pe)
                for k in range(VT):
                    ins = pe.transpose(side[:, 3, NS * k:NS * (k + 1)], hs[:, P * k:P * (k + 1)], ident[0:NS, 0:NS])
                ins.then_inc(hst_ready, 1)

            pe.wait_ge(conv_ready, 1)
            for j in range(KT):
                for g in range(2):
                    ins = mm(side[:, 2 + g, 0:HALF], ones[:, :], u[:, j, HALF * g:HALF * (g + 1)], j == 0, j == KT - 1)
            ins.then_inc(mean_ready, 1)

            def alternate(i, k, c0, s0, xhi, xlo):
                w = ring(i, 4, c0 + k)
                free(k % 2, 2 * i + (s0 + k // 2))
                product(k % 2, w, xhi, xlo).then_inc(chunk_done, 1)

            with pe.Fori(0, KT // 4) as i:
                for k in range(4):
                    alternate(i, k, C_GATE, S_GATE, ahi, alo)
            pe.wait_ge(sq_added, 2 * KT)
            column_sums(sqs, 0).then_inc(stat_ready, 1)
            with pe.Fori(0, KT // 4) as i:
                for k in range(4):
                    alternate(i, k, C_GATE + KT, S_GATE + KT // 2, ahi, alo)
            pe.wait_ge(opnd_lo, 2 * KT)
            with pe.Fori(0, KT // 4) as i:
                for k in range(4):
                    alternate(i, k, C_CONV, S_CONV, bhi, blo)

            def double(i, k, c0, s0, xhi, xlo):
                w = ring(i, 4, c0 + k)
                s = k // 2
                if k % 2 == 0:
                    free(s, i + s0)
                product(s, w, xhi, xlo, k % 2 == 0, k % 2 == 1, KT * (k % 2)).then_inc(chunk_done, 1)

            pe.wait_ge(mem_lo, 2 * KT)
            with pe.Fori(0, KT // 2) as i:
                for k in range(4):
                    double(i, k, C_MEM, S_MEM, mhi, mlo)
            pe.wait_ge(opnd_lo, 3 * KT)
            with pe.Fori(0, KT // 4) as i:
                for k in range(4):
                    alternate(i, k, C_OUT, S_OUT, bhi, blo)
            for n in (3, 4):
                pe.wait_ge(sq_added, n * KT)
                column_sums(sqs, 0).then_inc(stat_ready, 1)
            pe.wait_ge(opnd_lo, 4 * KT)
            for f in range(2):
                cf = C_FF + PERHALF * f
                sf = S_FF + S_HALF * f
                with pe.Fori(0, HID // 4) as i:
                    for k in range(4):
                        alternate(i, k, cf, sf, ahi, alo)
                pe.wait_ge(hid_lo, HID * (f + 1))
                with pe.Fori(0, KT // 2) as i:
                    for k in range(4):
                        double(i, k, cf + HID, sf + HID // 2, hidhi, hidlo)
            pe.wait_ge(sq_added, 5 * KT)
            column_sums(sqs, 0).then_inc(stat_ready, 1)


def kernel(x_prompt, x_sample, state_conv, state_C, state_n, state_m, g_pre_mix, w_in, b_in, w_dw, b_dw, g_cln, b_cln,
           w_conv_out, g_mh, w_m_out, w_o, g_post_mix, g_pre_ff, w_ff1, b_ff1, w_ff2, b_ff2, g_post_ff):
    import numpy as np
    import concourse.bacc as bacc
    from concourse.bass_utils import run_bass_kernel_spmd

    arr = lambda a: np.asarray(a)
    w, bi = arr(w_in)[0], arr(b_in)[0]
    o_ua, o_ug, o_q, o_k, o_v = 0, 1024, 2048, 3072, 4096
    o_o, o_ig, o_fg, o_gc, o_gm = 6144, 8192, 8196, 8200, 9224

    def chunks(m, rows=0):
        m = m[rows:rows + D_MODEL]
        return m.reshape(KT, P, m.shape[1] // P, P).transpose(2, 1, 0, 3)

    pair = lambda a, b: np.stack([a, b], axis=1).reshape((-1,) + a.shape[1:])
    parts = [pair(chunks(w[:, o_ug:o_q]), chunks(w[:, o_ua:o_ug]))]
    for h in range(HEADS):
        parts += [chunks(w[:, o_q + DK * h:o_q + DK * (h + 1)]), chunks(w[:, o_k + DK * h:o_k + DK * (h + 1)]),
                  chunks(w[:, o_v + DV * h:o_v + DV * (h + 1)]), chunks(w[:, o_o + DV * h:o_o + DV * (h + 1)])]
    parts += [chunks(w[:, o_gm:o_gm + D_MODEL]), chunks(w[:, o_gc:o_gm]), chunks(arr(w_conv_out)[0])]
    mo = arr(w_m_out)[0]
    parts += [pair(chunks(mo), chunks(mo, D_MODEL)), chunks(arr(w_o)[0])]
    ff1, ff2 = arr(w_ff1)[0], arr(w_ff2)[0]
    for f in range(2):
        parts += [chunks(ff1[:, HID * P * f:HID * P * (f + 1)]),
                  pair(chunks(ff2, HID * P * f), chunks(ff2, HID * P * f + D_MODEL))]
    wstream = np.concatenate(parts)

    feat = lambda v: v.reshape(-1, P).T
    cols = np.concatenate([feat(v) for v in (
        bi[o_ug:o_q], bi[o_ua:o_ug], bi[o_q:o_k], bi[o_k:o_v], bi[o_o:o_ig], bi[o_gc:o_gm], bi[o_gm:],
        arr(b_dw)[0], arr(g_cln)[0], arr(b_cln)[0], arr(g_pre_mix)[0], arr(g_mh)[0], arr(g_post_mix)[0],
        arr(g_pre_ff)[0], arr(b_ff1)[0], arr(b_ff2)[0], arr(g_post_ff)[0])], axis=1)
    w_gates = np.zeros((P, KT, 36), np.float32)
    w_gates[:, :, 0:4] = w[:, o_ig:o_fg].reshape(KT, P, 4).transpose(1, 0, 2)
    w_gates[:, :, 32:36] = w[:, o_fg:o_gc].reshape(KT, P, 4).transpose(1, 0, 2)
    b_gates = np.zeros((36, 1), np.float32)
    b_gates[0:4, 0] = bi[o_ig:o_fg]
    b_gates[32:36, 0] = bi[o_fg:o_gc]
    tokens = np.concatenate([arr(x_prompt)[0], arr(x_sample).reshape(NS, D_MODEL)])
    ins = dict(
        xT=tokens.T.reshape(KT, P, TT).transpose(1, 0, 2), wstream=wstream, w_gates=w_gates, cols=cols, b_gates=b_gates,
        b_v=bi[o_v:o_o].reshape(HEADS, DV), w_dw=arr(w_dw)[0].T.reshape(KT, P, WIDTH).transpose(1, 0, 2),
        hist=arr(state_conv)[0].transpose(2, 0, 1).reshape(KT, P, DEC_B, HIST).transpose(1, 0, 2, 3),
        c_in=arr(state_C)[0].transpose(1, 0, 3, 2).reshape(HEADS * DEC_B, QT, P, DV).transpose(0, 2, 1, 3),
        n_in=arr(state_n)[0].reshape(DEC_B, HEADS, QT, P).transpose(3, 1, 2, 0),
        m_in=arr(state_m)[0].T)
    outs = dict(yT=(P, KT, TT), conv_p=(P, KT, HIST), conv_s=(P, KT, DEC_B, HIST), c_p=(HEADS, VT, P, DK), n_p=(P, HEADS, QT),
                m_p=(HEADS, 1), c_s=(HEADS * DEC_B, P, QT, DV), n_s=(P, HEADS, QT, DEC_B), m_s=(HEADS, NS))

    nc = bacc.Bacc("TRN2", target_bir_lowering=False, num_devices=1, dynamic_dma_scratch_size=4096)
    arrays, aps = {}, {}
    for name, a in ins.items():
        arrays["in_" + name] = np.ascontiguousarray(a)
        aps[name] = nc.dram_tensor("in_" + name, a.shape, mybir.dt.float32, kind="ExternalInput").ap()
    for name, shape in outs.items():
        aps[name] = nc.dram_tensor("out_" + name, shape, mybir.dt.float32, kind="ExternalOutput").ap()
    hybrid_layer(nc, **aps)
    r = run_bass_kernel_spmd(nc, [arrays], core_ids=[0]).results[0]
    got = {name: np.asarray(r["out_" + name]) for name in outs}

    y = got["yT"].transpose(1, 0, 2).reshape(D_MODEL, TT).T
    conv_of_p = got["conv_p"].transpose(2, 1, 0).reshape(1, 1, HIST, D_MODEL)
    conv_of_s = got["conv_s"].transpose(2, 3, 1, 0).reshape(1, DEC_B, HIST, D_MODEL)
    c_of_s = got["c_s"].transpose(0, 2, 1, 3).reshape(HEADS, DEC_B, DK, DV).transpose(1, 0, 3, 2)
    return (y[:SEQ].reshape(1, SEQ, D_MODEL), y[SEQ:].reshape(DEC_B, DEC_T, D_MODEL),
            conv_of_p, got["c_p"].reshape(1, 1, HEADS, DV, DK), got["n_p"].transpose(1, 2, 0).reshape(1, 1, HEADS, DK),
            got["m_p"].reshape(1, 1, HEADS), conv_of_s, c_of_s.reshape(1, DEC_B, HEADS, DV, DK),
            got["n_s"].transpose(3, 1, 2, 0).reshape(1, DEC_B, HEADS, DK), got["m_s"][:, DEC_T - 1::DEC_T].T.reshape(1, DEC_B, HEADS))
```

```python
import concourse.bass as bass
from concourse import mybir
from contextlib import ExitStack

P = 128
D_MODEL = 1024
KT = D_MODEL // P
SEQ = 512
DEC_B, DEC_T = 8, 4
NS = DEC_B * DEC_T
TT = SEQ + NS
HALF = TT // 2
WIDTH = 31
HIST = WIDTH - 1
SROW = HIST + DEC_T
UCOLS = HIST + SEQ + DEC_B * SROW
HEADS = 4
DV, DK = 512, 256
VT, QT = DV // P, DK // P
ST = SEQ // P
EPS = 1e-6
RING = 4
C_RING = 4
HID = 16
PERHEAD = 2 * QT + 2 * VT

C_GLU = 0
C_HEAD = C_GLU + 2 * KT
C_GATE = C_HEAD + HEADS * PERHEAD
C_CONV = C_GATE + 2 * KT
C_MEM = C_CONV + KT
C_OUT = C_MEM + 2 * KT
C_FF = C_OUT + KT
PERHALF = HID + 2 * KT
N_CHUNKS = C_FF + 2 * PERHALF

USES = ["q0", "q1", "k0", "k1", "v0", "kts", "v1", "v2", "v3", "v4",
        "o0", "cu0", "cu1", "o1", "cu2", "cu3", "o2", "cu4", "cu5", "o3", "cu6", "cu7",
        "pv0", "pv1", "pv2", "pv3", "cc01", "cc23"]
USES_HEAD = len(USES) // 2
BY_CHUNK = {"q0": 0, "q1": 1, "k0": 2, "k1": 3, "v4": 7, "o0": 8, "o1": 9, "o2": 10, "o3": 11}
BY_SLOT = [[n for n in USES[s::2] if n not in BY_CHUNK] for s in range(2)]
S_HEAD = KT
S_GATE = S_HEAD + HEADS * USES_HEAD
S_CONV = S_GATE + KT
S_MEM = S_CONV + KT // 2
S_OUT = S_MEM + KT // 2
S_FF = S_OUT + KT // 2
S_HALF = HID // 2 + KT // 2

COLS = {}
_at = 0
for _name, _n in (("b_ug", 8), ("b_ua", 8), ("b_q", 8), ("b_k", 8), ("b_o", 16), ("b_gc", 8), ("b_gm", 8),
                  ("b_dw", 8), ("g_cln", 8), ("b_cln", 8), ("g_pre_mix", 8), ("g_mh", 16), ("g_post_mix", 8),
                  ("g_pre_ff", 8), ("b_ff1", 32), ("b_ff2", 8), ("g_post_ff", 8)):
    COLS[_name] = _at
    _at += _n
N_COLS = _at

R_NEGM, R_M, R_WINTER, R_WK, R_DEC = 0, TT, 2 * TT, 2 * TT + NS, 2 * TT + 2 * NS
N_ROW = R_DEC + DEC_B

PT_AT = [0, 512, 896, 1152, 1280]
N_PT = 1280 + NS
ST_AT = [(0, 0), (1, 0), (2, 0), (1, 384), (2, 256)]

V_TAPS = [(5, 8), (8, 11), (11, 13), (13, 15)]
C_TAPS = [(17, 19), (19, 19), (19, 21), (21, 22), (22, 24), (24, 25), (25, 26), (26, 27)]
DVE_PER_HEAD = 146


class Steps:

    def __init__(self):
        self.n, self.off = 0, 0

    def loop(self, i, per):
        self.start, self.per, self.off = self.n, per, i * per

    def leave(self, turns):
        assert self.n - self.start == self.per, (self.n - self.start, self.per)
        self.n, self.off = self.start + self.per * turns, 0

    def add(self):
        self.n += 1
        return self.off + self.n


def hybrid_layer(nc, xT, wstream, w_gates, cols, b_gates, b_v, w_dw, hist, c_in, n_in, m_in,
                 yT, conv_p, conv_s, c_p, n_p, m_p, c_s, n_s, m_s):
    f32, f32r = mybir.dt.float32, mybir.dt.float32r
    ALU = mybir.AluOpType
    ACT = mybir.ActivationFunctionType
    X = mybir.AxisListType.X
    rows_dram = nc.dram_tensor("head_rows", (HEADS, N_ROW), f32, kind="Internal").ap()

    ctx = ExitStack()
    with ctx:
        cursor = [4224]

        def at(name, shape, dt, where=None):
            size = 4
            for n in shape[1:]:
                size *= n
            size = (size + 31) // 32 * 32
            where_ = cursor[0] if where is None else where
            t = nc.alloc_sbuf_tensor_at(name, shape, dt, offset=where_)
            if where is None:
                cursor[0] += size
            assert max(cursor[0], where_ + size) <= 229344, (name, cursor[0])
            return t

        wraw = at("wraw", [P, 2, KT, P], f32)
        whi = at("whi", [P, RING, KT, P], f32r)
        wlo = at("wlo", [P, RING, KT, P], f32r)
        col = at("col", [P, N_COLS], f32)
        wdw = at("wdw", [P, KT, WIDTH], f32)
        ones = at("ones", [P, P], f32)
        ident = at("ident", [P, P], f32)
        causal = at("causal", [P, P], f32)
        causal_s = at("causal_s", [NS, DEC_B, DEC_T], f32)
        own = at("own", [NS, DEC_B], f32)
        nold = at("nold", [P, HEADS, QT, DEC_B], f32)
        nnew = at("nnew", [P, HEADS, QT, DEC_B], f32)
        npn = at("npn", [P, HEADS, QT], f32)
        eps = at("eps", [P, 1], f32)
        warm = at("warm", [P, 1], f32)
        acol = at("acol", [P, ST + 1, HEADS], f32)
        wkcol = at("wkcol", [NS, HEADS], f32)
        mcol = at("mcol", [NS, HEADS], f32)
        asmp = at("asmp", [P, KT, 2, NS], f32r, cursor[0])
        rst = at("rst", [P, TT], f32)
        xa0 = cursor[0]
        ahi = at("ahi", [P, KT, TT], f32r)
        alo = at("alo", [P, KT, TT], f32r)
        mhi = at("mhi", [P, 2 * KT, TT], f32r, xa0)
        hm0 = cursor[0]
        hm = at("hm", [P, 2 * KT, TT], f32)
        mlo = at("mlo", [P, 2 * KT, TT], f32r, hm0)
        x0 = at("x0", [P, KT, TT], f32, hm0)
        g0 = hm0 + KT * TT * 4
        wg = at("wg", [P, KT, 36], f32, g0)
        wghi = at("wghi", [P, KT, 36], f32r, g0 + KT * 36 * 4)
        wglo = at("wglo", [P, KT, 36], f32r, g0 + 2 * KT * 36 * 4)
        hidhi = at("hidhi", [P, HID, TT], f32r, hm0)
        u0 = cursor[0]
        u = at("u", [P, KT, UCOLS], f32)
        y = at("y", [P, KT, TT], f32, u0)
        tmp0 = cursor[0]
        vtok = at("vtok", [P, ST + 1, DV], f32)
        pt = at("pt", [P, N_PT], f32)
        kw = at("kw", [P, ST, DK], f32)
        hs0 = cursor[0]
        hs = at("hs", [NS, DV], f32)
        kwh = at("kwh", [NS, DK], f32r, hs0)
        kwl = at("kwl", [NS, DK], f32, hs0 + DK * 4)
        qT = at("qT", [P, QT, TT], f32)
        kT = at("kT", [P, QT, TT], f32)
        hb = at("hb", [P, N_ROW], f32)
        wkp = at("wkp", [P, ST], f32)
        bv = at("bv", [P, DV], f32, cursor[0])
        hr = at("hr", [P, 2, SEQ], f32)
        sg = at("sg", [P, TT], f32, cursor[0])
        sqh = at("sqh", [P, 2, SEQ], f32)
        sqacc = at("sqacc", [P, SEQ], f32)
        rden = at("rden", [P, SEQ], f32)
        qm = at("qm", [P, QT, DEC_B * 36], f32)
        qn = at("qn", [P, QT, NS], f32)
        kn = at("kn", [P, QT, NS], f32)
        nd = at("nd", [P, QT, DEC_B], f32)
        kr = at("kr", [P, QT, DEC_B], f32)
        kws = at("kws", [NS, DK], f32, cursor[0])
        hsq = at("hsq", [NS, DV], f32, cursor[0])
        cst = at("cst", [P, VT, DK], f32, cursor[0])
        kst = at("kst", [96, DEC_B, DK], f32r)
        vst = at("vst", [96, DV], f32r)
        sst = at("sst", [NS, 8], f32)
        accp = at("accp", [P, 2, SEQ], f32)
        accs = at("accs", [P, 2, NS], f32)
        crg = at("crg", [P, C_RING, QT, DV], f32)
        rw = tmp0
        row = {}
        for name in ("ig", "fg", "ex", "B", "a", "M", "one"):
            row[name] = at("row_" + name, [HEADS, TT], f32, rw)
            rw += TT * 4
        rout = at("rout", [HEADS, N_ROW], f32, rw)
        rw += N_ROW * 4
        m0 = at("m0", [HEADS, DEC_B], f32, rw)
        bg = at("bg", [36, 1], f32, rw + 32)
        assert rw + 64 <= hs0 + DV * 4
        late = tmp0
        bhi = at("bhi", [P, KT, TT], f32r, late)
        blo = at("blo", [P, KT, TT], f32r, late + KT * TT * 4)
        hidlo = at("hidlo", [P, HID, TT], f32r, late)
        late += 2 * KT * TT * 4
        yc = at("yc", [P, KT, TT], f32, late)
        late += KT * TT * 4
        sgm = at("sgm", [P, KT, TT], f32, late)
        late += KT * TT * 4
        fr = at("fr", [P, 4, TT], f32, late)
        late += 4 * TT * 4
        sqs = at("sqs", [P, TT], f32, late)
        mu = at("mu", [P, TT], f32, tmp0)

        psum = [ctx.enter_context(nc.psum_tensor(f"product{s}", [P, 2, 512], f32)) for s in range(2)]
        side = ctx.enter_context(nc.psum_tensor("side", [P, 4, 512], f32))

        def tok(ap):
            return ap.rearrange("p (a n) -> p a n", a=2)

        def sem(name):
            return ctx.enter_context(nc.semaphore(name))

        x_in = [sem(f"x_in{s}") for s in range(KT // 2)]
        const_in, gate_in, hist_in = sem("const_in"), sem("gate_in"), sem("hist_in")
        raw_in = [sem(f"raw_in{s}") for s in range(2)]
        hb_in, bv_in, x2_in = sem("hb_in"), sem("bv_in"), sem("x2_in")
        c_loaded = [sem(f"c_loaded{s}") for s in range(C_RING)]
        c_saved = [sem(f"c_saved{s}") for s in range(C_RING)]
        rows_out, conv_saved, cst_saved, small_saved, out_saved = (sem(n) for n in (
            "rows_out", "conv_saved", "cst_saved", "small_saved", "out_saved"))
        hi_done, lo_done, chunk_done = sem("hi_done"), sem("lo_done"), sem("chunk_done")
        ready = [sem(f"ready{s}") for s in range(2)]
        drained = [sem(f"drained{s}") for s in range(2)]
        pool_step, dve_step, ex_ready = sem("pool_step"), sem("dve_step"), sem("ex_ready")
        sq_ready, sq_added, stat_ready = sem("sq_ready"), sem("sq_added"), sem("stat_ready")
        ms_ready, root_ready, table_in = sem("ms_ready"), sem("root_ready"), sem("table_in")
        asmp_ready = sem("asmp_ready")
        tile_ready, opnd_hi, opnd_lo = sem("tile_ready"), sem("opnd_hi"), sem("opnd_lo")
        gw_hi, gw_lo, gates_ready, fx_ready, ln_ready, rex_ready, rex_done, rows_ready, rowT_ready, rowT_used = (
            sem(n) for n in ("gw_hi", "gw_lo", "gates_ready", "fx_ready", "ln_ready", "rex_ready", "rex_done",
                             "rows_ready", "rowT_ready", "rowT_used"))
        u_done, head_done = sem("u_done"), sem("head_done")
        kt_ready, kt_used = sem("kt_ready"), sem("kt_used")
        st_ready, w_diag, w_ready, pt_ready = sem("st_ready"), sem("w_diag"), sem("w_ready"), sem("pt_ready")
        expm_ready, wkp_ready, vs_hi, vs_all, kh_ready, ops_ready = (sem(n) for n in (
            "expm_ready", "wkp_ready", "vs_hi", "vs_all", "kh_ready", "ops_ready"))
        den_ready, den_abs, sden_ready, sden_abs = sem("den_ready"), sem("den_abs"), sem("sden_ready"), sem("sden_abs")
        snum_ready, hs_ready, hs_sq, hs_var, hs_std, hs_norm, hst_ready, hst_used = (sem(n) for n in (
            "snum_ready", "hs_ready", "hs_sq", "hs_var", "hs_std", "hs_norm", "hst_ready", "hst_used"))
        hsq_ready, hsum_ready, ss_ready, var_ready, std_ready = (sem(n) for n in (
            "hsq_ready", "hsum_ready", "ss_ready", "var_ready", "std_ready"))
        kl_ready, kst_ready = sem("kl_ready"), sem("kst_ready")
        np_ready, np_used, nn_ready = sem("np_ready"), sem("np_used"), sem("nn_ready")
        conv_ready, mean_ready, xc_ready, cn_ready, csg_ready = (sem(n) for n in (
            "conv_ready", "mean_ready", "xc_ready", "cn_ready", "csg_ready"))
        mem_hi, mem_lo, mixed, y_scaled = sem("mem_hi"), sem("mem_lo"), sem("mixed"), sem("y_scaled")
        x1_ready = [sem(f"x1_ready{s}") for s in range(2)]
        hidsq_ready, hid_hi, hid_lo = sem("hidsq_ready"), sem("hid_hi"), sem("hid_lo")
        out_ready = [sem(f"out_ready{s}") for s in range(2)]
        block = ctx.enter_context(nc.Block())

        def c(name, j):
            return col[:, bass.ds(COLS[name] + j, 1)]

        def tile(buf, j, lo=0, n=TT):
            return buf[:, bass.ds(j, 1), lo:lo + n]

        def wait_filled(eng, h, name):
            s = USES.index(name) % 2
            if name in BY_CHUNK:
                eng.wait_ge(chunk_done, PERHEAD * h + (C_HEAD + BY_CHUNK[name] + 1))
            else:
                eng.wait_ge(ready[s], len(BY_SLOT[s]) * h + (BY_SLOT[s].index(name) + 1))
            return s

        def wait_drained(eng, h, name):
            n = USES.index(name)
            eng.wait_ge(drained[n % 2], USES_HEAD * h + (S_HEAD + n // 2 + 1))

        def apart(eng):
            eng.nop(nofuse=True)

        def halves(ap):
            return ap.rearrange("p a (s n) -> p (a s) n", s=2)

        def slot(s):
            return psum[s][:, :, 0:HALF]

        @block.sync
        def _(sp):
            stream = wstream.rearrange("(n s) p k m -> n s p k m", s=2)
            for q in range(KT // 2):
                sp.dma_start(x0[:, 2 * q:2 * q + 2, :], xT[:, 2 * q:2 * q + 2, :]).then_inc(x_in[q], 16)
            sp.dma_start(col[:, :], cols).then_inc(const_in, 16)
            sp.dma_start(wg[:, :, :], w_gates).then_inc(gate_in, 16)
            sp.dma_start(bg[:, :], b_gates).then_inc(gate_in, 16)
            sp.dma_start(m0[:, :], m_in).then_inc(gate_in, 16)
            for s in range(2):
                sp.dma_start(wraw[:, s, :, :], wstream[s, :, :, :]).then_inc(raw_in[s], 16)
            sp.dma_start(wdw[:, :, :], w_dw).then_inc(const_in, 16)
            sp.dma_start(nold[:, :, :, :], n_in).then_inc(const_in, 16)

            def load(first, last):
                with sp.Fori(first, last) as i:
                    for s in range(2):
                        sp.wait_ge(lo_done, 2 * i + (s - 1))
                        sp.dma_start(wraw[:, s, :, :],
                                     stream[bass.ds(i, 1), s, :, :, :].rearrange("a p k m -> p (a k) m")).then_inc(raw_in[s], 16)

            load(1, (C_OUT + 4) // 2)
            sp.wait_ge(mixed, KT)
            sp.dma_start(sgm[:, :, :], xT).then_inc(x2_in, 16)
            load((C_OUT + 4) // 2, N_CHUNKS // 2)
            for j in range(KT):
                sp.wait_ge(out_ready[j % 2], j // 2 + 1)
                sp.dma_start(yT[:, j, :], y[:, j, :]).then_inc(out_saved, 16)
            sp.wait_ge(out_saved, 16 * KT)
            sp.wait_ge(conv_saved, 16 * 2 * KT)
            sp.wait_ge(small_saved, 16 * 4)
            sp.wait_ge(cst_saved, 16 * HEADS)
            for s in range(C_RING):
                sp.wait_ge(c_saved[s], 16 * (DEC_B // C_RING) * HEADS)

        @block.gpsimd
        def _(pool):
            pool.memset(eps[:, :], EPS).then_inc(pool_step, 1)
            pool.memset(ones[:, :], 1.0).then_inc(pool_step, 1)
            pool.memset(ident[:, :], 0.0).then_inc(pool_step, 1)
            pool.memset(causal[:, :], 0.0).then_inc(pool_step, 1)
            pool.memset(causal_s[:, :, :], 0.0).then_inc(pool_step, 1)
            pool.memset(own[:, :], 1.0).then_inc(pool_step, 1)
            pool.memset(u[:, :, 0:HIST], 0.0).then_inc(pool_step, 1)
            pool.memset(qm[:, :, :], 0.0).then_inc(pool_step, 1)
            pool.memset(row["one"][:, :], 1.0).then_inc(pool_step, 1)
            pool.wait_ge(pool_step, 9)
            pool.affine_select(out=ident[:, :], in_=ident[:, :], compare_op=ALU.not_equal, fill=1.0, base=0,
                               pattern=[[-1, P]], channel_multiplier=1).then_inc(pool_step, 1)
            pool.affine_select(out=causal[:, :], in_=causal[:, :], compare_op=ALU.is_ge, fill=-1e30, base=0,
                               pattern=[[1, P]], channel_multiplier=-1).then_inc(pool_step, 1)
            pool.affine_select(out=causal_s[:, :, :], in_=causal_s[:, :, :], compare_op=ALU.is_ge, fill=-1e30, base=0,
                               pattern=[[DEC_T, DEC_B], [1, DEC_T]], channel_multiplier=-1).then_inc(pool_step, 1)
            pool.wait_ge(pool_step, 12)
            pool.affine_select(out=causal_s[:, :, :], in_=causal_s[:, :, :], compare_op=ALU.is_ge, fill=-1e30, base=0,
                               pattern=[[-DEC_T, DEC_B], [0, DEC_T]], channel_multiplier=1).then_inc(pool_step, 1)
            pool.affine_select(out=own[:, :], in_=own[:, :], compare_op=ALU.is_ge, fill=0.0, base=0,
                               pattern=[[-DEC_T, DEC_B]], channel_multiplier=1).then_inc(pool_step, 1)
            pool.wait_ge(pool_step, 14)
            pool.affine_select(out=own[:, :], in_=own[:, :], compare_op=ALU.is_ge, fill=0.0, base=DEC_T - 1,
                               pattern=[[DEC_T, DEC_B]], channel_multiplier=-1).then_inc(pool_step, 1)
            for ct in range(KT):
                dst = u[:, ct, HIST + SEQ:].rearrange("p (b r) -> p b r", r=SROW)[:, :, 0:HIST]
                pool.dma_start(dst, hist[:, ct, :, :]).then_inc(hist_in, 16)
            pool.wait_ge(rows_ready, 1)
            pool.dma_start(rows_dram, rout[:, :]).then_inc(rows_out, 16)
            pool.dma_start(m_p, rout[:, R_M + SEQ - 1:R_M + SEQ]).then_inc(small_saved, 16)
            pool.dma_start(m_s, rout[:, R_M + SEQ:R_M + TT]).then_inc(small_saved, 16)
            pool.wait_ge(rows_out, 16)
            c_in5 = c_in.rearrange("(h b) p k v -> h b p k v", h=HEADS)
            c_s5 = c_s.rearrange("(h b) p k v -> h b p k v", h=HEADS)

            def rows_load(h):
                pool.dma_start(hb[:, :], rows_dram[bass.ds(h, 1), :].broadcast_to([P, N_ROW])).then_inc(hb_in, 16)

            def bias_load(h):
                pool.dma_start(bv[:, :], b_v[bass.ds(h, 1), :].broadcast_to([P, DV])).then_inc(bv_in, 16)

            def state_load(h, b):
                s = b % C_RING
                pool.dma_start(crg[:, s, :, :], c_in5[bass.ds(h, 1), b, :, :, :].rearrange("a p k v -> p (a k) v")).then_inc(c_loaded[s], 16)

            def state_saved(h, b):
                pool.wait_ge(c_saved[b % C_RING], 16 * (DEC_B // C_RING) * h + 16 * (b // C_RING + 1))

            def states(h):
                for b in range(DEC_B):
                    wait_drained(pool, h, f"cu{b}")
                    apart(pool)
                    s = b % C_RING
                    pool.dma_start(c_s5[bass.ds(h, 1), b, :, :, :].rearrange("a p k v -> p (a k) v"), crg[:, s, :, :]).then_inc(c_saved[s], 16)
                    if 1 <= b and b - 1 + C_RING < DEC_B:
                        state_saved(h, b - 1)
                        state_load(h, b - 1 + C_RING)

            def prompt_state(h):
                for name in ("cc01", "cc23"):
                    wait_drained(pool, h, name)
                apart(pool)
                pool.dma_start(c_p[bass.ds(h, 1), :, :, :].rearrange("a v p k -> p (a v) k"), cst[:, :, :]).then_inc(cst_saved, 16)

            rows_load(0)
            bias_load(0)
            for b in range(C_RING):
                state_load(0, b)
            pool.wait_ge(u_done, 2 * KT)
            pool.wait_ge(drained[1], KT)
            pool.wait_ge(hist_in, 16 * KT)
            for ct in range(KT):
                pool.dma_start(conv_p[:, ct, :], u[:, ct, SEQ:SEQ + HIST]).then_inc(conv_saved, 16)
                src = u[:, ct, HIST + SEQ:].rearrange("p (b r) -> p b r", r=SROW)[:, :, DEC_T:SROW]
                pool.dma_start(conv_s[:, ct, :, :], src).then_inc(conv_saved, 16)
            with pool.Fori(0, HEADS - 1) as h:
                states(h)
                rows_load(h + 1)
                for b in range(C_RING):
                    state_saved(h, b + DEC_B - C_RING)
                    state_load(h + 1, b)
                prompt_state(h)
                pool.wait_ge(cst_saved, 16 * h + 16)
                pool.wait_ge(head_done, h + 1)
                bias_load(h + 1)
            states(HEADS - 1)
            prompt_state(HEADS - 1)
            pool.wait_ge(nn_ready, 2 * HEADS)
            pool.dma_start(n_s, nnew[:, :, :, :]).then_inc(small_saved, 16)
            pool.wait_ge(np_used, HEADS)
            pool.dma_start(n_p, npn[:, :, :]).then_inc(small_saved, 16)
            pool.wait_ge(x2_in, 16)
            for n in range(2):
                for j in range(1, KT, 2):
                    pool.wait_ge(y_scaled, KT * n + j + 1)
                    if n == 0:
                        pool.tensor_tensor(yc[:, j, :], y[:, j, :], sgm[:, j, :], ALU.add).then_inc(x1_ready[1], 1)
                    else:
                        pool.tensor_tensor(y[:, j, :], y[:, j, :], yc[:, j, :], ALU.add).then_inc(out_ready[1], 1)

        @block.scalar
        def _(act):
            def hi(i, per, k):
                act.wait_ge(raw_in[k % 2], 8 * per * i + 16 * (k // 2 + 1))
                if k >= RING:
                    act.wait_ge(chunk_done, per * i + (k - RING + 1))
                act.activation(whi[:, k % RING, :, :], wraw[:, k % 2, :, :], ACT.Copy).then_inc(hi_done, 1)

            def squares(n, src, k, depth=2):
                if not isinstance(n, int) or n >= depth:
                    act.wait_ge(sq_added, n - (depth - 1))
                if not isinstance(n, int):
                    apart(act)
                act.activation(fr[:, k:k + 1, :], src, ACT.Square).then_inc(sq_ready, 1)

            def root(n, sums, count):
                if n > 1:
                    act.wait_ge(table_in, n - 1)
                act.activation(warm[:, :], eps[:, :], ACT.Ln).then_inc(table_in, 1)
                act.wait_ge(sums, count)
                act.activation(tok(rst[:, :]), side[:, 0:2, 0:HALF], ACT.Ln, bias=eps[:, :], scale=1.0 / D_MODEL).then_inc(ms_ready, 1)
                act.wait_ge(ms_ready, n)
                act.activation(rst[:, :], rst[:, :], ACT.Exp, scale=-0.5).then_inc(root_ready, 1)

            def operand(j, n, dst):
                act.wait_ge(tile_ready, n + 1)
                act.activation(tile(dst, j), fr[:, 2 + j % 2:3 + j % 2, :], ACT.Copy).then_inc(opnd_hi, 1)

            for j in range(KT):
                act.wait_ge(x_in[j // 2], 16)
                squares(j, tile(x0, j), j % 4, 4)
            for k in range(2):
                hi(0, 4, k)
            act.wait_ge(pool_step, 15)
            root(1, sq_added, KT)
            for j in range(KT):
                if j == 4:
                    hi(0, 4, 2)
                operand(j, j, ahi)
            act.wait_ge(gate_in, 48)
            act.activation(wghi[:, :, :], wg[:, :, :], ACT.Copy).then_inc(gw_hi, 1)

            def glu(i):
                for k in range(4):
                    hi(i, 4, k + 3)
                    if k % 2 == 0:
                        j = 2 * i + k // 2
                        act.wait_ge(chunk_done, 4 * i + k + 1)
                        if k > 0:
                            act.wait_ge(drained[1], j)
                        act.activation(halves(sg[:, :].rearrange("p (a t) -> p a t", a=1)), slot(0), ACT.Sigmoid,
                                       bias=c("b_ug", j)).then_inc(drained[0], 1)
                act.wait_ge(drained[1], 2 * i + 2)
                act.wait_ge(chunk_done, 4 * i + 4)

            glu(0)
            act.wait_ge(opnd_lo, KT)
            for q, part in enumerate((ahi, alo)):
                act.activation(asmp[:, :, q, :], part[:, :, SEQ:TT].bitcast(f32), ACT.Copy).then_inc(asmp_ready, 1)
            act.wait_ge(fx_ready, 1)
            act.activation(row["ex"][:, :], row["ex"][:, :], ACT.Exp).then_inc(ex_ready, 1)
            act.wait_ge(ex_ready, 1)
            act.activation(row["ex"][:, :], row["ex"][:, :], ACT.Ln, bias=1.0).then_inc(ln_ready, 1)
            act.wait_ge(rex_ready, 3)
            act.activation(rout[:, R_WINTER:N_ROW], rout[:, R_WINTER:N_ROW], ACT.Exp).then_inc(rex_done, 1)
            with act.Fori(1, KT // 2) as i:
                glu(i)

            act.wait_ge(rowT_ready, 1)
            for s in range(ST + 1):
                n = P if s < ST else NS
                act.activation(acol[0:n, s, :], side[0:n, 3, 4 * s:4 * s + 4], ACT.Copy).then_inc(rowT_used, 1)
            act.activation(wkcol[:, :], side[0:NS, 3, 20:24], ACT.Copy).then_inc(rowT_used, 1)
            act.activation(mcol[:, :], side[0:NS, 3, 24:28], ACT.Exp, scale=-1.0).then_inc(rowT_used, 1)
            act.wait_ge(const_in, 48)
            with act.Fori(0, HEADS) as h:
                def use(name):
                    return wait_filled(act, h, name)

                def was_drained(name):
                    wait_drained(act, h, name)

                def split(k):
                    hi(h, PERHEAD, C_HEAD + k)

                split(3)
                split(4)
                act.wait_ge(hb_in, 16 * h + 16)
                act.activation(hb[:, R_M:R_M + SEQ], hb[:, R_M:R_M + SEQ], ACT.Exp, scale=-1.0).then_inc(expm_ready, 1)
                act.wait_ge(rowT_used, ST + 3)
                act.activation(wkp[:, :], acol[:, 0:ST, bass.ds(h, 1)].rearrange("p s a -> p (s a)"), ACT.Exp,
                               bias=hb[:, R_NEGM + SEQ - 1:R_NEGM + SEQ]).then_inc(wkp_ready, 1)
                for s in range(ST - 1):
                    act.activation(pt[:, PT_AT[s] + P:PT_AT[s] + SEQ - P * s], hb[:, R_NEGM + P * (s + 1):R_NEGM + SEQ],
                                   ACT.Exp, bias=acol[:, s, bass.ds(h, 1)]).then_inc(w_ready, 1)
                split(5)
                s = use("k0")
                act.activation(halves(kT[:, 0:1, :]), slot(s), ACT.Identity, bias=c("b_k", 2 * h)).then_inc(drained[s], 1)
                split(6)
                split(7)
                s = use("k1")
                act.activation(halves(kT[:, 1:2, :]), slot(s), ACT.Identity, bias=c("b_k", 2 * h + 1)).then_inc(drained[s], 1)
                act.wait_ge(w_diag, 5 * h + 5)
                apart(act)
                for s in range(ST):
                    d = pt[:, PT_AT[s]:PT_AT[s] + P]
                    act.activation(d, d, ACT.Exp, bias=acol[:, s, bass.ds(h, 1)]).then_inc(w_ready, 1)
                d = pt[0:NS, PT_AT[ST]:N_PT]
                act.activation(d, d, ACT.Exp, bias=acol[0:NS, ST, bass.ds(h, 1)]).then_inc(w_ready, 1)
                was_drained("kts")
                act.activation(kwh[:, :], kws[:, :], ACT.Copy).then_inc(kh_ready, 1)
                act.wait_ge(kh_ready, h + 1)
                act.wait_ge(kl_ready, h + 1)
                apart(act)
                for q in range(3):
                    part = kwl[:, :] if q == 2 else kwh[:, :].bitcast(f32)
                    for b in range(DEC_B):
                        act.activation(kst[NS * q:NS * (q + 1), b, :], part, ACT.Copy, scale=own[:, b:b + 1]).then_inc(kst_ready, 1)
                act.wait_ge(wkp_ready, h + 1)
                for half in range(2):
                    act.wait_ge(kt_ready, 2 * h + (half + 1))
                    for q in (2 * half, 2 * half + 1):
                        act.activation(kw[:, q, :], side[:, half, DK * (q % 2):DK * (q % 2 + 1)], ACT.Copy,
                                       scale=wkp[:, q:q + 1]).then_inc(kt_used, 1)
                split(8)
                was_drained("v4")
                act.activation(vst[0:NS, :], vtok[0:NS, ST, :], ACT.Copy).then_inc(vs_hi, 1)
                act.activation(vst[64:96, :], vtok[0:NS, ST, :], ACT.Copy).then_inc(vs_all, 1)
                split(9)
                split(10)
                for k in range(VT):
                    split(11 + k)
                    s = use(f"o{k}")
                    act.activation(halves(tile(hm, 4 * h + k)), slot(s), ACT.Sigmoid, bias=c("b_o", 4 * h + k)).then_inc(drained[s], 1)
                    if k == 0:
                        act.wait_ge(den_ready, h + 1)
                        act.activation(rden[:, :], side[:, 0, :], ACT.Abs).then_inc(den_abs, 1)
                        act.wait_ge(sden_ready, h + 1)
                        act.activation(sst[:, 0:1], side[0:NS, 2, 0:1], ACT.Abs).then_inc(sden_abs, 1)
                act.wait_ge(hs_ready, h + 1)
                act.activation(hsq[:, :], hs[:, :], ACT.Square, accum_out=sst[:, 2:3]).then_inc(hs_sq, 1)
                for k in range(VT):
                    was_drained(f"pv{k}")
                    if k == 3:
                        act.wait_ge(hsum_ready, 3 * h + 1)
                    dst = sqacc[:, :] if k == 0 else sqh[:, k % 2, :]
                    act.activation(dst, hr[:, k % 2, :], ACT.Square).then_inc(hsq_ready, 1)
                act.wait_ge(hs_sq, h + 1)
                act.activation(sst[:, 3:4], sst[:, 2:3], ACT.Ln, bias=eps[0:NS, :], scale=1.0 / DV).then_inc(hs_var, 1)
                act.wait_ge(hs_var, h + 1)
                act.activation(sst[:, 4:5], sst[:, 3:4], ACT.Exp, scale=-0.5).then_inc(hs_std, 1)
                act.wait_ge(np_ready, h + 1)
                act.activation(npn[:, bass.ds(h, 1), :], side[:, 2:3, P:P + QT], ACT.Copy).then_inc(np_used, 1)
                for half in range(2):
                    s = use(("cc01", "cc23")[half])
                    act.activation(cst[:, 2 * half:2 * half + 2, :].rearrange("p a k -> p (a k)"), psum[s][:, 0, :],
                                   ACT.Copy).then_inc(drained[s], 1)
                act.wait_ge(ss_ready, h + 1)
                act.activation(sqacc[:, :], side[:, 1, :], ACT.Ln, bias=eps[:, :], scale=1.0 / DV).then_inc(var_ready, 1)
                act.wait_ge(var_ready, h + 1)
                act.activation(sqacc[:, :], sqacc[:, :], ACT.Exp, scale=-0.5).then_inc(std_ready, 1)

            act.wait_ge(head_done, HEADS)
            act.wait_ge(cst_saved, 16 * HEADS)
            for s in range(C_RING):
                act.wait_ge(c_saved[s], 16 * (DEC_B // C_RING) * HEADS)
            with act.Fori(0, KT // 4) as i:
                for k in range(4):
                    hi(i, 4, C_GATE + k + 3)
                    j = 4 * i + k
                    act.wait_ge(chunk_done, 4 * i + (C_GATE + k + 1))
                    act.activation(halves(tile(sgm, j)), slot(k % 2), ACT.Sigmoid, bias=c("b_gm", j)).then_inc(drained[k % 2], 1)
                    act.wait_ge(xc_ready, j + 1)
                    squares(j + KT, tile(u, j), k % 2)
            root(2, stat_ready, 1)
            with act.Fori(0, KT // 4) as i:
                for k in range(4):
                    hi(i, 4, C_GATE + KT + k + 3)
                    j = 4 * i + k
                    act.wait_ge(cn_ready, j + 1)
                    apart(act)
                    act.activation(fr[:, k % 2:k % 2 + 1, :], tile(u, j), ACT.Sigmoid, bias=c("b_cln", j)).then_inc(csg_ready, 1)
                    act.wait_ge(tile_ready, KT + j + 1)
                    apart(act)
                    act.activation(tile(bhi, j), tile(u, j), ACT.Copy).then_inc(opnd_hi, 1)
                    act.wait_ge(chunk_done, 4 * i + (C_GATE + KT + k + 1))
                    act.activation(halves(tile(yc, j)), slot(k % 2), ACT.Sigmoid, bias=c("b_gc", j)).then_inc(drained[k % 2], 1)
            with act.Fori(0, KT // 4) as i:
                for k in range(4):
                    hi(i, 4, C_CONV + k + 3)
                    if k == 0:
                        act.wait_ge(chunk_done, C_CONV)
                        apart(act)
                    for q in range(2):
                        act.activation(tile(mhi, 8 * i + 2 * k + q), tile(hm, 8 * i + 2 * k + q), ACT.Copy).then_inc(mem_hi, 1)
            with act.Fori(0, KT // 2) as i:
                for k in range(4):
                    hi(i, 4, C_MEM + k + 3)
                    if k % 2 == 1:
                        j = 2 * i + k // 2
                        act.wait_ge(mixed, j + 1)
                        apart(act)
                        act.activation(tile(bhi, j), tile(yc, j), ACT.Copy).then_inc(opnd_hi, 1)
            with act.Fori(0, KT // 4) as i:
                for k in range(4):
                    hi(i, 4, C_OUT + k + 3)
                    j = 4 * i + k
                    act.wait_ge(chunk_done, 4 * i + (C_OUT + k + 1))
                    act.activation(halves(tile(y, j)), slot(k % 2), ACT.Copy).then_inc(drained[k % 2], 1)
                    act.wait_ge(drained[k % 2], 2 * i + (S_OUT + k // 2 + 1))
                    squares(j + 2 * KT, tile(y, j), k % 2)
            root(3, stat_ready, 2)
            for j in range(KT):
                act.wait_ge(x1_ready[j % 2], j // 2 + 1)
                squares(3 * KT + j, tile(yc, j), j % 4, 4)
            root(4, sq_added, 4 * KT)
            for j in range(KT):
                operand(j, 2 * KT + j, ahi)
            for f in range(2):
                cf = C_FF + PERHALF * f
                sf = S_FF + S_HALF * f
                with act.Fori(0, HID // 4) as i:
                    for k in range(4):
                        hi(i, 4, cf + k + 3)
                        n = HID * f + k + 1
                        act.wait_ge(drained[k % 2], 2 * i + (sf + k // 2 + 1))
                        act.activation(fr[:, 2 + k % 2, :], fr[:, k % 2, :], ACT.Square).then_inc(hidsq_ready, 1)
                        act.wait_ge(hidsq_ready, 4 * i + n)
                        act.activation(tile(hidhi, 4 * i + k), fr[:, 2 + k % 2:3 + k % 2, :], ACT.Copy).then_inc(hid_hi, 1)

                def down(i, ks):
                    for k in range(4):
                        if k in ks:
                            hi(i, 4, cf + HID + k + 3)
                        if k % 2 == 1:
                            j = 2 * i + k // 2
                            if f == 0:
                                act.wait_ge(chunk_done, 4 * i + (cf + HID + k + 1))
                                act.activation(halves(tile(sgm, j)), slot(k // 2), ACT.Identity, bias=c("b_ff2", j)).then_inc(drained[k // 2], 1)
                            else:
                                act.wait_ge(drained[k // 2], i + (sf + HID // 2 + 1))
                                squares(4 * KT + j, tile(y, j), k // 2)

                turns = KT // 2 - f
                with act.Fori(0, turns) as i:
                    down(i, range(4))
                if f == 1:
                    down(turns, range(1))
            root(5, stat_ready, 3)

        @block.vector
        def _(dve):
            V = nc.vector
            st = Steps()

            def mark(ins):
                ins.then_inc(dve_step, 1)
                return st.add()

            def lo(i, per, k):
                dve.wait_ge(hi_done, per * i + (k + 1))
                V.tensor_tensor(wlo[:, k % RING, :, :], wraw[:, k % 2, :, :], whi[:, k % RING, :, :].bitcast(f32),
                                ALU.subtract).then_inc(lo_done, 1)

            def add_square(n, k, base=None):
                dve.wait_ge(sq_ready, n + 1)
                if base is None:
                    dve.wait_ge(sq_added, n)
                V.tensor_tensor(sqs[:, :], sqs[:, :], fr[:, k, :], ALU.add).then_inc(sq_added, 1)

            rst3 = rst[:, :].rearrange("p (a t) -> p a t", a=1)

            def operands(m, src, gain, dst_hi, dst_lo, between=()):
                def make(j):
                    if j >= 2:
                        dve.wait_ge(opnd_lo, m + j - 1)
                    V.scalar_tensor_tensor(fr[:, 2 + j % 2:3 + j % 2, :], tile(src, j), c(gain, j), rst3, ALU.mult,
                                           ALU.mult).then_inc(tile_ready, 1)

                make(0)
                for j in range(KT):
                    if j + 1 < KT:
                        make(j + 1)
                    dve.wait_ge(opnd_hi, m + j + 1)
                    V.tensor_tensor(tile(dst_lo, j), fr[:, 2 + j % 2:3 + j % 2, :], tile(dst_hi, j).bitcast(f32),
                                    ALU.subtract).then_inc(opnd_lo, 1)
                    if j in between:
                        between[j]()

            for k in range(2):
                lo(0, 4, k)
            dve.wait_ge(const_in, 16 * 3)
            dve.wait_ge(root_ready, 1)
            operands(0, x0, "g_pre_mix", ahi, alo, {3: lambda: lo(0, 4, 2)})
            dve.wait_ge(gw_hi, 1)
            V.tensor_tensor(wglo[:, :, :], wg[:, :, :], wghi[:, :, :].bitcast(f32), ALU.subtract).then_inc(gw_lo, 1)

            def glu(i):
                for k in range(4):
                    lo(i, 4, k + 3)
                    if k % 2 == 1:
                        j = 2 * i + k // 2
                        dve.wait_ge(chunk_done, 4 * i + k + 1)
                        dve.wait_ge(drained[0], j + 1)
                        V.scalar_tensor_tensor(tile(u, j, HIST, HALF), psum[1][:, 0:1, 0:HALF], c("b_ua", j),
                                               sg[:, 0:HALF].rearrange("p (a t) -> p a t", a=1), ALU.add, ALU.mult).then_inc(u_done, 1)
                        V.scalar_tensor_tensor(tile(u, j, HIST + HALF, SEQ - HALF), psum[1][:, 1:2, 0:SEQ - HALF], c("b_ua", j),
                                               sg[:, HALF:SEQ].rearrange("p (a t) -> p a t", a=1), ALU.add, ALU.mult).then_inc(u_done, 1)
                        new = tile(u, j, HIST + SEQ, DEC_B * SROW).rearrange("p a (b r) -> p (a b) r", r=SROW)[:, :, HIST:SROW]
                        V.scalar_tensor_tensor(new, psum[1][:, 1, SEQ - HALF:HALF].rearrange("p (b t) -> p b t", t=DEC_T),
                                               c("b_ua", j), sg[:, SEQ:TT].rearrange("p (b t) -> p b t", t=DEC_T),
                                               ALU.add, ALU.mult).then_inc(drained[1], 1)

            glu(0)
            dve.wait_ge(gates_ready, 1)
            dve.wait_ge(gate_in, 48)
            dve.wait_ge(pool_step, 15)
            r2 = lambda name: row[name][:, :].rearrange("p (a n) -> p a n", a=2)
            n = mark(V.tensor_scalar(r2("fg"), side[32:36, 0:2, 0:HALF], bg[32:36, :], None, ALU.add))
            dve.wait_ge(dve_step, n)
            V.scalar_tensor_tensor(row["ex"][:, :], row["fg"][:, :], -1.0, row["fg"][:, :], ALU.mult, ALU.min).then_inc(fx_ready, 1)
            ig = mark(V.tensor_scalar(r2("ig"), side[0:4, 0:2, 0:HALF], bg[0:4, :], None, ALU.add))
            dve.wait_ge(ln_ready, 1)
            lf = mark(V.scalar_tensor_tensor(row["fg"][:, :], row["fg"][:, :], 0.0, row["ex"][:, :], ALU.min, ALU.subtract))
            dve.wait_ge(dve_step, lf)
            mark(V.tensor_tensor_scan(row["B"][:, 0:SEQ], row["one"][:, 0:SEQ], row["fg"][:, 0:SEQ], 0.0, ALU.mult, ALU.add))
            seq = lambda name: row[name][:, SEQ:TT].rearrange("h (b t) -> h b t", t=DEC_T)
            n = mark(V.tensor_copy(seq("B")[:, :, 0], seq("fg")[:, :, 0]))
            for t in range(1, DEC_T):
                dve.wait_ge(dve_step, n)
                n = mark(V.tensor_tensor(seq("B")[:, :, t], seq("B")[:, :, t - 1], seq("fg")[:, :, t], ALU.add))
            dve.wait_ge(dve_step, n)
            n = mark(V.tensor_tensor(row["a"][:, :], row["ig"][:, :], row["B"][:, :], ALU.subtract))
            dve.wait_ge(dve_step, n)
            mark(V.tensor_tensor_scan(row["M"][:, 0:SEQ], row["a"][:, 0:SEQ], row["a"][:, 0:SEQ], 0.0, ALU.max, ALU.max))
            n = mark(V.tensor_tensor(seq("M")[:, :, 0], seq("a")[:, :, 0], m0[:, :], ALU.max))
            for t in range(1, DEC_T):
                dve.wait_ge(dve_step, n)
                n = mark(V.tensor_tensor(seq("M")[:, :, t], seq("M")[:, :, t - 1], seq("a")[:, :, t], ALU.max))
            dve.wait_ge(dve_step, n)
            mark(V.tensor_tensor(rout[:, R_M:R_M + TT], row["B"][:, :], row["M"][:, :], ALU.add))
            mark(V.tensor_scalar(rout[:, R_NEGM:R_NEGM + TT], row["M"][:, :], -1.0, None, ALU.mult))
            last = seq("M")[:, :, DEC_T - 1]
            V.tensor_tensor(rout[:, R_WINTER:R_WK].rearrange("h (b t) -> h b t", t=DEC_T),
                            m0[:, :].rearrange("h (b a) -> h b a", a=1).broadcast_to([HEADS, DEC_B, DEC_T]), seq("M"),
                            ALU.subtract).then_inc(rex_ready, 1)
            V.tensor_tensor(rout[:, R_WK:R_DEC].rearrange("h (b t) -> h b t", t=DEC_T), seq("a"),
                            seq("M")[:, :, DEC_T - 1:DEC_T].broadcast_to([HEADS, DEC_B, DEC_T]), ALU.subtract).then_inc(rex_ready, 1)
            V.tensor_tensor(rout[:, R_DEC:N_ROW], m0[:, :], last, ALU.subtract).then_inc(rex_ready, 1)
            dve.wait_ge(rex_done, 1)
            dve.wait_ge(dve_step, st.n)
            V.tensor_copy(row["one"][:, 0:4], row["one"][:, 4:8]).then_inc(rows_ready, 1)

            with dve.Fori(1, KT // 2) as i:
                glu(i)

            dve.wait_ge(hist_in, 16 * KT)
            dve.wait_ge(rowT_used, ST + 3)
            dve.wait_ge(rows_out, 16)
            dve.wait_ge(small_saved, 32)
            dve.wait_ge(u_done, 2 * KT)
            dve.wait_ge(drained[1], KT)
            with dve.Fori(0, HEADS) as h:
                st.loop(h, DVE_PER_HEAD)
                hh = bass.ds(h, 1)

                def use(name):
                    return wait_filled(dve, h, name)

                def was_drained(name):
                    wait_drained(dve, h, name)

                def split(k):
                    lo(h, PERHEAD, C_HEAD + k)

                def taps(first, last):
                    for tap in range(first, last):
                        for q in range(2):
                            w = wdw[:, bass.ds(2 * h + q, 1), tap].rearrange("p a -> p (a)")
                            src = tile(u, 2 * h + q, tap, SEQ)
                            ssrc = tile(u, 2 * h + q, HIST + SEQ, DEC_B * SROW).rearrange("p a (b r) -> p (a b) r", r=SROW)[:, :, tap:tap + DEC_T]
                            ap, sp_ = accp[:, q:q + 1, :], accs[:, q, :].rearrange("p (b t) -> p b t", t=DEC_T)
                            for kind, (sum_, rows) in enumerate(((ap, src), (sp_, ssrc))):
                                if tap == 0:
                                    ins = V.tensor_scalar(sum_, rows, w, c("b_dw", 2 * h + q), ALU.mult, ALU.add)
                                else:
                                    dve.wait_ge(dve_step, conv_at[2 * q + kind])
                                    ins = V.scalar_tensor_tensor(sum_, rows, w, sum_, ALU.mult, ALU.add)
                                conv_at[2 * q + kind] = mark(ins)

                conv_at = [0] * 4
                split(3)
                s = use("q0")
                V.tensor_scalar(halves(qT[:, 0:1, :]), slot(s), c("b_q", 2 * h), DK ** -0.5, ALU.add, ALU.mult).then_inc(drained[s], 1)
                taps(0, 2)
                split(4)
                s = use("q1")
                V.tensor_scalar(halves(qT[:, 1:2, :]), slot(s), c("b_q", 2 * h + 1), DK ** -0.5, ALU.add, ALU.mult).then_inc(drained[s], 1)
                dve.wait_ge(hb_in, 16 * h + 16)
                for s in range(ST):
                    V.tensor_tensor(pt[:, PT_AT[s]:PT_AT[s] + P], hb[:, R_NEGM + P * s:R_NEGM + P * (s + 1)], causal[:, :],
                                    ALU.add).then_inc(w_diag, 1)
                V.tensor_tensor(pt[0:NS, PT_AT[ST]:N_PT], hb[0:NS, R_NEGM + SEQ:R_NEGM + TT],
                                causal_s[:, :, :].rearrange("s b t -> s (b t)"), ALU.add).then_inc(w_diag, 1)
                was_drained("q0")
                was_drained("q1")
                qd = [qm[:, kk, :].rearrange("p (b c) -> p b c", c=36)[:, :, 0:DEC_T] for kk in range(QT)]
                for kk in range(QT):
                    V.tensor_tensor(qd[kk], qT[:, kk, SEQ:TT].rearrange("p (b t) -> p b t", t=DEC_T),
                                    hb[:, R_WINTER:R_WK].rearrange("p (b t) -> p b t", t=DEC_T), ALU.mult).then_inc(ops_ready, 1)
                split(5)
                dve.wait_ge(ops_ready, 5 * h + 2)
                for kk in range(QT):
                    V.tensor_tensor(qn[:, kk, :].rearrange("p (b t) -> p b t", t=DEC_T), qd[kk],
                                    nold[:, hh, kk, :].rearrange("p a (b c) -> p (a b) c", c=1).broadcast_to([P, DEC_B, DEC_T]),
                                    ALU.mult).then_inc(ops_ready, 1)
                split(6)
                taps(2, 4)
                split(7)
                was_drained("k1")
                n = 0
                for kk in range(QT):
                    n = mark(V.tensor_tensor(kn[:, kk, :], kT[:, kk, SEQ:TT], hb[:, R_WK:R_DEC], ALU.mult))
                for kk in range(QT):
                    n = mark(V.tensor_tensor(nd[:, kk, :], nold[:, hh, kk, :].rearrange("p a b -> p (a b)"), hb[:, R_DEC:N_ROW], ALU.mult))
                dve.wait_ge(dve_step, n)
                for kk in range(QT):
                    n = mark(V.tensor_reduce(kr[:, kk, :], kn[:, kk, :].rearrange("p (b t) -> p b t", t=DEC_T), X, ALU.add))
                dve.wait_ge(dve_step, n)
                for kk in range(QT):
                    V.tensor_tensor(nnew[:, hh, kk, :].rearrange("p a b -> p (a b)"), nd[:, kk, :], kr[:, kk, :], ALU.add).then_inc(nn_ready, 1)
                taps(4, 5)
                dve.wait_ge(bv_in, 16 * h + 16)
                for s_ in range(ST + 1):
                    s = use(f"v{s_}")
                    if s_ < ST:
                        V.tensor_tensor(vtok[:, s_, :], psum[s][:, 0, :], bv[:, :], ALU.add).then_inc(drained[s], 1)
                    else:
                        n = mark(V.tensor_tensor(vtok[0:NS, ST, :], psum[s][0:NS, 0, :], bv[0:NS, :], ALU.add))
                        dve.wait_ge(dve_step, n)
                        V.tensor_tensor(vtok[0:NS, ST, :], psum[s][NS:2 * NS, 0, :], vtok[0:NS, ST, :], ALU.add).then_inc(drained[s], 1)
                    if s_ == 0:
                        s = use("kts")
                        V.tensor_scalar(kws[:, :], psum[s][0:NS, 0, 0:DK], wkcol[:, hh], None, ALU.mult).then_inc(drained[s], 1)
                        dve.wait_ge(kh_ready, h + 1)
                        V.tensor_tensor(kwl[:, :], kws[:, :], kwh[:, :].bitcast(f32), ALU.subtract).then_inc(kl_ready, 1)
                    if s_ < ST:
                        taps(*V_TAPS[s_])
                split(8)
                dve.wait_ge(vs_hi, h + 1)
                V.tensor_tensor(vst[NS:2 * NS, :], vtok[0:NS, ST, :], vst[0:NS, :].bitcast(f32), ALU.subtract).then_inc(ops_ready, 1)
                taps(15, 17)
                dve.wait_ge(st_ready, 5 * h + 5)
                for s in range(ST + 1):
                    dve.wait_ge(w_ready, 8 * h + ST + s)
                    bank, at_ = ST_AT[s]
                    n_, w_ = (P, SEQ - P * s) if s < ST else (NS, NS)
                    d = pt[0:n_, PT_AT[s]:PT_AT[s] + w_]
                    V.tensor_tensor(d, d, side[0:n_, bank, at_:at_ + w_], ALU.mult).then_inc(pt_ready, 1)
                split(9)
                split(10)
                for k in range(VT):
                    split(11 + k)
                    if k == 0:
                        dve.wait_ge(den_abs, h + 1)
                        dve.wait_ge(expm_ready, h + 1)
                        n = mark(V.tensor_tensor(rden[:, :], rden[:, :], hb[:, R_M:R_M + SEQ], ALU.max))
                        dve.wait_ge(sden_abs, h + 1)
                        n2 = mark(V.tensor_tensor(sst[:, 0:1], sst[:, 0:1], mcol[:, hh], ALU.max))
                    for b in (2 * k, 2 * k + 1):
                        s = use(f"cu{b}")
                        V.scalar_tensor_tensor(crg[:, b % C_RING, :, :], crg[:, b % C_RING, :, :], hb[:, R_DEC + b:R_DEC + b + 1],
                                               psum[s][:, :, :], ALU.mult, ALU.add).then_inc(drained[s], 1)
                        if b == 1:
                            dve.wait_ge(dve_step, n2)
                            n = mark(V.reciprocal(rden[:, :], rden[:, :]))
                            n2 = mark(V.reciprocal(sst[:, 1:2], sst[:, 0:1]))
                        else:
                            taps(*C_TAPS[b])
                dve.wait_ge(snum_ready, h + 1)
                dve.wait_ge(dve_step, n2)
                V.tensor_scalar(hs[:, :], side[0:NS, 3, :], sst[:, 1:2], None, ALU.mult).then_inc(hs_ready, 1)
                dve.wait_ge(dve_step, n)
                for k in range(VT):
                    s = use(f"pv{k}")
                    if k >= 2:
                        dve.wait_ge(hsq_ready, VT * h + (k - 1))
                    V.tensor_tensor(hr[:, k % 2, :], psum[s][:, 0, :], rden[:, :], ALU.mult).then_inc(drained[s], 1)
                    was_drained(f"pv{k}")
                    d = tile(hm, 4 * h + k, 0, SEQ)
                    n = mark(V.tensor_tensor(d, d, hr[:, k % 2:k % 2 + 1, :], ALU.mult))
                    if k >= 1:
                        dve.wait_ge(hsq_ready, VT * h + (k + 1))
                        if k >= 2:
                            dve.wait_ge(hsum_ready, 3 * h + (k - 1))
                        V.tensor_tensor(sqacc[:, :], sqacc[:, :], sqh[:, k % 2, :], ALU.add).then_inc(hsum_ready, 1)
                taps(27, 29)
                dve.wait_ge(hs_std, h + 1)
                V.tensor_scalar(hs[:, :], hs[:, :], sst[:, 4:5], None, ALU.mult).then_inc(hs_norm, 1)
                taps(29, WIDTH)
                dve.wait_ge(conv_saved, 16 * 2 * KT)
                dve.wait_ge(dve_step, conv_at[3])
                apart(dve)
                for q in range(2):
                    mark(V.tensor_copy(tile(u, 2 * h + q, 0, SEQ), accp[:, q:q + 1, :]))
                    m = mark(V.tensor_copy(tile(u, 2 * h + q, SEQ, NS), accs[:, q:q + 1, :]))
                dve.wait_ge(hst_ready, h + 1)
                for k in range(VT):
                    d = tile(hm, 4 * h + k, SEQ, NS)
                    V.scalar_tensor_tensor(d, side[:, 3:4, NS * k:NS * (k + 1)], c("g_mh", 4 * h + k), d, ALU.mult,
                                           ALU.mult).then_inc(hst_used, 1)
                dve.wait_ge(std_ready, h + 1)
                dve.wait_ge(dve_step, m)
                apart(dve)
                for k in range(VT):
                    d = tile(hm, 4 * h + k, 0, SEQ)
                    ins = V.scalar_tensor_tensor(d, d, c("g_mh", 4 * h + k), sqacc[:, :].rearrange("p (a t) -> p a t", a=1), ALU.mult, ALU.mult)
                    if k < VT - 1:
                        mark(ins)
                    else:
                        ins.then_inc(head_done, 1)
            st.leave(HEADS)

            dve.wait_ge(head_done, HEADS)
            dve.wait_ge(cst_saved, 16 * HEADS)
            for s in range(C_RING):
                dve.wait_ge(c_saved[s], 16 * (DEC_B // C_RING) * HEADS)
            dve.wait_ge(dve_step, st.n)
            V.memset(sqs[:, :], 0.0).then_inc(conv_ready, 1)
            dve.wait_ge(mean_ready, 1)
            n = mark(V.tensor_scalar(mu[:, :].rearrange("p (a n) -> p a n", a=2), side[:, 2:4, 0:HALF], 1.0 / D_MODEL, None, ALU.mult))
            dve.wait_ge(dve_step, n)
            dve.wait_ge(conv_ready, 1)
            with dve.Fori(0, KT // 4) as i:
                for k in range(4):
                    lo(i, 4, C_GATE + k + 3)
                    j = 4 * i + k
                    V.tensor_tensor(tile(u, j, 0, TT), tile(u, j, 0, TT), mu[:, :].rearrange("p (a t) -> p a t", a=1),
                                    ALU.subtract).then_inc(xc_ready, 1)
                    add_square(KT + j, k % 2)
            dve.wait_ge(root_ready, 2)
            with dve.Fori(0, KT // 4) as i:
                for k in range(4):
                    j = 4 * i + k
                    V.scalar_tensor_tensor(tile(u, j), tile(u, j), c("g_cln", j), rst3, ALU.mult, ALU.mult).then_inc(cn_ready, 1)
                    lo(i, 4, C_GATE + KT + k + 3)
                    dve.wait_ge(csg_ready, j + 1)
                    V.scalar_tensor_tensor(tile(u, j), tile(u, j), c("b_cln", j), fr[:, k % 2:k % 2 + 1, :], ALU.add, ALU.mult).then_inc(tile_ready, 1)
                    dve.wait_ge(opnd_hi, KT + j + 1)
                    V.tensor_tensor(tile(blo, j), tile(u, j), tile(bhi, j).bitcast(f32), ALU.subtract).then_inc(opnd_lo, 1)
            with dve.Fori(0, KT // 4) as i:
                for k in range(4):
                    lo(i, 4, C_CONV + k + 3)
                    j = 4 * i + k
                    for q in range(2):
                        m = 8 * i + 2 * k + q
                        dve.wait_ge(mem_hi, m + 1)
                        V.tensor_tensor(tile(mlo, m), tile(hm, m), tile(mhi, m).bitcast(f32), ALU.subtract).then_inc(mem_lo, 1)
                    dve.wait_ge(chunk_done, 4 * i + (C_CONV + k + 1))
                    V.tensor_tensor(halves(tile(yc, j)), slot(k % 2), halves(tile(yc, j)), ALU.mult).then_inc(drained[k % 2], 1)
            with dve.Fori(0, KT // 2) as i:
                for k in range(4):
                    lo(i, 4, C_MEM + k + 3)
                    if k % 2 == 1:
                        s, j = k // 2, 2 * i + k // 2
                        dve.wait_ge(chunk_done, 4 * i + (C_MEM + k + 1))
                        V.tensor_tensor(halves(fr[:, s:s + 1, :]), slot(s), halves(tile(sgm, j)), ALU.mult).then_inc(drained[s], 1)
                        dve.wait_ge(drained[s], i + (S_MEM + 1))
                        V.tensor_tensor(tile(yc, j), tile(yc, j), fr[:, s:s + 1, :], ALU.add).then_inc(mixed, 1)
                        dve.wait_ge(opnd_hi, 2 * KT + j + 1)
                        V.tensor_tensor(tile(blo, j), tile(yc, j), tile(bhi, j).bitcast(f32), ALU.subtract).then_inc(opnd_lo, 1)
            dve.wait_ge(sq_added, 2 * KT)
            n = mark(V.memset(sqs[:, :], 0.0))
            dve.wait_ge(dve_step, n)
            with dve.Fori(0, KT // 4) as i:
                for k in range(4):
                    lo(i, 4, C_OUT + k + 3)
                    dve.wait_ge(sq_ready, 4 * i + (2 * KT + k + 1))
                    dve.wait_ge(sq_added, 4 * i + (2 * KT + k))
                    V.tensor_tensor(sqs[:, :], sqs[:, :], fr[:, k % 2, :], ALU.add).then_inc(sq_added, 1)
            dve.wait_ge(root_ready, 3)
            def scaled(gain, j):
                V.scalar_tensor_tensor(tile(y, j), tile(y, j), c(gain, j), rst3, ALU.mult, ALU.mult).then_inc(y_scaled, 1)

            dve.wait_ge(x2_in, 16)
            for j in range(0, KT, 2):
                scaled("g_post_mix", j)
                scaled("g_post_mix", j + 1)
                dve.wait_ge(y_scaled, j + 1)
                V.tensor_tensor(tile(yc, j), tile(y, j), tile(sgm, j), ALU.add).then_inc(x1_ready[0], 1)
            dve.wait_ge(root_ready, 4)
            for s in range(2):
                dve.wait_ge(x1_ready[s], KT // 2)
            operands(3 * KT, yc, "g_pre_ff", ahi, alo)
            n = mark(V.memset(sqs[:, :], 0.0))
            dve.wait_ge(dve_step, n)
            for f in range(2):
                cf = C_FF + PERHALF * f
                sf = S_FF + S_HALF * f
                with dve.Fori(0, HID // 4) as i:
                    for k in range(4):
                        lo(i, 4, cf + k + 3)
                        n = HID * f + k + 1
                        dve.wait_ge(chunk_done, 4 * i + (cf + k + 1))
                        V.tensor_scalar(halves(fr[:, k % 2:k % 2 + 1, :]), slot(k % 2), c("b_ff1", 4 * i + (HID * f + k)), 0.0,
                                        ALU.add, ALU.max).then_inc(drained[k % 2], 1)
                        dve.wait_ge(hid_hi, 4 * i + n)
                        V.tensor_tensor(tile(hidlo, 4 * i + k), fr[:, 2 + k % 2:3 + k % 2, :], tile(hidhi, 4 * i + k).bitcast(f32),
                                        ALU.subtract).then_inc(hid_lo, 1)

                def down(i, ks):
                    for k in range(4):
                        if k in ks:
                            lo(i, 4, cf + HID + k + 3)
                        if k % 2 == 1 and f == 1:
                            s, j = k // 2, 2 * i + k // 2
                            dve.wait_ge(chunk_done, 4 * i + (cf + HID + k + 1))
                            V.tensor_tensor(halves(tile(y, j)), slot(s), halves(tile(sgm, j)), ALU.add).then_inc(drained[s], 1)
                            dve.wait_ge(sq_ready, j + (4 * KT + 1))
                            dve.wait_ge(sq_added, j + 4 * KT)
                            V.tensor_tensor(sqs[:, :], sqs[:, :], fr[:, s, :], ALU.add).then_inc(sq_added, 1)

                turns = KT // 2 - f
                with dve.Fori(0, turns) as i:
                    down(i, range(4))
                if f == 1:
                    down(turns, range(1))
            dve.wait_ge(root_ready, 5)
            for j in range(0, KT, 2):
                scaled("g_post_ff", j)
                scaled("g_post_ff", j + 1)
                dve.wait_ge(y_scaled, KT + j + 1)
                V.tensor_tensor(tile(y, j), tile(y, j), tile(yc, j), ALU.add).then_inc(out_ready[0], 1)

        @block.tensor
        def _(pe):
            def mm(out, lhsT, rhs, start, stop, check=False):
                return pe.matmul(out, lhsT, rhs, start=start, stop=stop, skip_group_check=check)

            def part(s, w, xhi, xlo, kt, first=True, last=True, x_at=0):
                for n, (a, b) in enumerate(((whi, xhi), (whi, xlo), (wlo, xhi))):
                    for g in range(2):
                        ins = mm(psum[s][:, g, 0:HALF], a[:, w, kt, :], b[:, x_at + kt, HALF * g:HALF * (g + 1)],
                                 first and kt == 0 and n == 0, last and kt == KT - 1 and n == 2)
                return ins

            def product(s, w, xhi, xlo, first=True, last=True, x_at=0, arrive=None):
                for kt in range(KT):
                    if arrive is not None:
                        pe.wait_ge(arrive[0], arrive[1] + kt + 1)
                    ins = part(s, w, xhi, xlo, kt, first, last, x_at)
                return ins

            def two_products(xhi, xlo, count):
                for kt in range(KT):
                    pe.wait_ge(opnd_lo, count + kt + 1)
                    for s in range(2):
                        ins = part(s, s, xhi, xlo, kt)
                        if kt == KT - 1:
                            ins.then_inc(chunk_done, 1)

            def sum_of_squares(n):
                for j in range(KT):
                    pe.wait_ge(sq_ready, n + j + 1)
                    for g in range(2):
                        ins = mm(side[:, g, 0:HALF], ones[:, :], fr[:, j % 4, HALF * g:HALF * (g + 1)], j == 0, j == KT - 1)
                    ins.then_inc(sq_added, 1)

            def ring(i, per, k):
                pe.wait_ge(lo_done, per * i + (k + 1))
                return k % RING

            def free(s, n):
                pe.wait_ge(drained[s], n)

            def column_sums(src, banks):
                for g in range(2):
                    ins = mm(side[:, banks + g, 0:HALF], ones[:, :], src[:, HALF * g:HALF * (g + 1)], True, True)
                return ins

            pe.wait_ge(pool_step, 15)
            sum_of_squares(0)

            def glu(i, k):
                s, j = k % 2, 2 * i + k // 2
                w = ring(i, 4, k)
                free(s, j)
                product(s, w, ahi, alo).then_inc(chunk_done, 1)

            ring(0, 4, 1)
            two_products(ahi, alo, 0)
            for k in range(2, 4):
                glu(0, k)
            pe.wait_ge(root_ready, 1)
            pe.wait_ge(gw_lo, 1)
            n = 0
            for kt in range(KT):
                for a, b in ((wghi, ahi), (wghi, alo), (wglo, ahi)):
                    for g in range(2):
                        ins = mm(side[0:36, g, 0:HALF], a[:, kt, :], b[:, kt, HALF * g:HALF * (g + 1)], n == 0, n == 3 * KT - 1)
                    n += 1
            ins.then_inc(gates_ready, 1)
            with pe.Fori(1, KT // 2) as i:
                for k in range(4):
                    glu(i, k)
            pe.wait_ge(rows_ready, 1)
            for s in range(ST + 1):
                n_ = P if s < ST else NS
                pe.transpose(side[0:n_, 3, 4 * s:4 * s + 4], row["a"][:, P * s:P * s + n_], ident[0:4, 0:4])
            pe.transpose(side[0:NS, 3, 20:24], rout[:, R_WK:R_DEC], ident[0:4, 0:4])
            pe.transpose(side[0:NS, 3, 24:28], rout[:, R_M + SEQ:R_M + TT], ident[0:4, 0:4]).then_inc(rowT_ready, 1)

            pe.wait_ge(asmp_ready, 2)
            with pe.Fori(0, HEADS) as h:
                def use(name):
                    n = USES.index(name)
                    free(n % 2, USES_HEAD * h + (S_HEAD + n // 2))
                    return n % 2

                def was_drained(name):
                    wait_drained(pe, h, name)

                def chunk(name, k):
                    w = ring(h, PERHEAD, C_HEAD + k)
                    s = use(name)
                    product(s, w, ahi, alo).then_inc(chunk_done, 1)

                for k, name in enumerate(("q0", "q1", "k0", "k1")):
                    chunk(name, k)
                def values(q, chunks):
                    s = USES.index(f"v{q}") % 2
                    n = 0
                    for kt in range(KT):
                        for a, b in ((whi, ahi), (whi, alo), (wlo, ahi)):
                            ins = mm(psum[s][:, 0, P * chunks.start:P * chunks.stop].rearrange("p (c m) -> p c m", m=P),
                                     b[:, kt, P * q:P * (q + 1)], a[:, chunks.start:chunks.stop, kt, :], n == 0, n == 3 * KT - 1)
                            n += 1
                    return ins

                s = use("v0")
                for places in (range(0, 2), range(2, 4)):
                    for k in places:
                        ring(h, PERHEAD, C_HEAD + 4 + k)
                    ins = values(0, places)
                ins.then_inc(ready[s], 1)
                was_drained("k1")
                s = use("kts")
                for kk in range(QT):
                    ins = pe.transpose(psum[s][0:NS, 0, P * kk:P * (kk + 1)], kT[:, kk, SEQ:TT], ident[:, :])
                ins.then_inc(ready[s], 1)
                was_drained("q0")
                was_drained("q1")
                apart(pe)
                for half in range(2):
                    for q in range(2):
                        for kk in range(QT):
                            t = P * (2 * half + q)
                            ins = pe.transpose(side[:, half, DK * q + P * kk:DK * q + P * (kk + 1)], kT[:, kk, t:t + P], ident[:, :])
                    ins.then_inc(kt_ready, 1)
                for q in range(1, ST):
                    s = use(f"v{q}")
                    values(q, range(4)).then_inc(ready[s], 1)
                s = use("v4")
                for kt in range(KT):
                    both = asmp[:, kt, :, :].rearrange("p a t -> p (a t)")
                    for a in (whi, wlo):
                        ins = mm(psum[s][0:2 * NS, 0, :].rearrange("p (c m) -> p c m", m=P), both, a[:, :, kt, :],
                                 kt == 0 and a is whi, kt == KT - 1 and a is wlo)
                ins.then_inc(chunk_done, 4)
                pe.wait_ge(kt_used, ST * h + ST)
                apart(pe)
                for q in range(ST + 1):
                    bank, at_ = ST_AT[q]
                    n_, w_ = (P, SEQ - P * q) if q < ST else (NS, NS)
                    for kk in range(QT):
                        ins = mm(side[0:n_, bank, at_:at_ + w_], kT[:, kk, P * q:P * q + n_], qT[:, kk, P * q:P * q + w_],
                                 kk == 0, kk == QT - 1)
                    ins.then_inc(st_ready, 1)
                for k in range(VT):
                    chunk(f"o{k}", 8 + k)
                    if k == 0:
                        pe.wait_ge(pt_ready, 5 * h + 5)
                        pe.wait_ge(ops_ready, 5 * h + 5)
                        pe.wait_ge(kst_ready, 3 * DEC_B * (h + 1))
                        for q in range(ST):
                            ins = mm(side[:, 0, P * q:SEQ], ones[:, :], pt[:, PT_AT[q]:PT_AT[q] + SEQ - P * q], q == 0, q == ST - 1)
                        ins.then_inc(den_ready, 1)
                        mm(side[0:NS, 2, 0:1], pt[0:NS, PT_AT[ST]:N_PT], ones[0:NS, 0:1], True, False)
                        for kk in range(QT):
                            ins = mm(side[0:NS, 2, 0:1], qn[:, kk, :], ones[:, 0:1], False, kk == QT - 1)
                        ins.then_inc(sden_ready, 1)
                        mm(side[0:NS, 3, :], pt[0:NS, PT_AT[ST]:N_PT], vtok[0:NS, ST, :], True, False)
                    pe.wait_ge(vs_all, h + 1)
                    for b in (2 * k, 2 * k + 1):
                        pe.wait_ge(c_loaded[b % C_RING], 16 * (DEC_B // C_RING) * h + 16 * (b // C_RING + 1))
                        for kk in range(QT):
                            ins = mm(side[0:NS, 3, :], qm[:, kk, NS * b:NS * (b + 1)], crg[:, b % C_RING, kk, :], False,
                                     b == DEC_B - 1 and kk == QT - 1)
                        if b == DEC_B - 1:
                            ins.then_inc(snum_ready, 1)
                        s = use(f"cu{b}")
                        for kk in range(QT):
                            ins = mm(psum[s][:, kk, :], kst[:, b, P * kk:P * (kk + 1)], vst[:, :], True, True)
                        ins.then_inc(ready[s], 1)
                for k in range(VT):
                    s = use(f"pv{k}")
                    for q in range(ST):
                        ins = mm(psum[s][:, 0, P * q:SEQ], vtok[:, q, P * k:P * (k + 1)], pt[:, PT_AT[q]:PT_AT[q] + SEQ - P * q],
                                 q == 0, q == ST - 1)
                    ins.then_inc(ready[s], 1)
                pe.wait_ge(sden_abs, h + 1)
                for kk in range(QT):
                    for q in range(ST):
                        ins = mm(side[:, 2, P + kk:P + kk + 1], kw[:, q, P * kk:P * (kk + 1)], ones[:, 0:1], q == 0, q == ST - 1)
                ins.then_inc(np_ready, 1)
                for half in range(2):
                    s = use(("cc01", "cc23")[half])
                    for r in range(2):
                        for q in range(ST):
                            v = P * (2 * half + r)
                            ins = mm(psum[s][:, 0, DK * r:DK * (r + 1)], vtok[:, q, v:v + P], kw[:, q, :], q == 0, q == ST - 1)
                    ins.then_inc(ready[s], 1)
                pe.wait_ge(hsum_ready, 3 * h + 3)
                mm(side[:, 1, :], ones[:, :], sqacc[:, :], True, True).then_inc(ss_ready, 1)
                pe.wait_ge(hs_norm, h + 1)
                apart(pe)
                for k in range(VT):
                    ins = pe.transpose(side[:, 3, NS * k:NS * (k + 1)], hs[:, P * k:P * (k + 1)], ident[0:NS, 0:NS])
                ins.then_inc(hst_ready, 1)

            def alternate(i, k, c0, s0, xhi, xlo, arrive=None):
                w = ring(i, 4, c0 + k)
                free(k % 2, 2 * i + (s0 + k // 2))
                product(k % 2, w, xhi, xlo, arrive=arrive).then_inc(chunk_done, 1)

            for k in range(4):
                alternate(0, k, C_GATE, S_GATE, ahi, alo)
                if k == 1:
                    pe.wait_ge(conv_ready, 1)
                    for j in range(KT):
                        for g in range(2):
                            ins = mm(side[:, 2 + g, 0:HALF], ones[:, :], u[:, j, HALF * g:HALF * (g + 1)], j == 0, j == KT - 1)
                    ins.then_inc(mean_ready, 1)
            with pe.Fori(1, KT // 4) as i:
                for k in range(4):
                    alternate(i, k, C_GATE, S_GATE, ahi, alo)
            pe.wait_ge(sq_added, 2 * KT)
            column_sums(sqs, 0).then_inc(stat_ready, 1)
            with pe.Fori(0, KT // 4) as i:
                for k in range(4):
                    alternate(i, k, C_GATE + KT, S_GATE + KT // 2, ahi, alo)
            with pe.Fori(0, KT // 4) as i:
                for k in range(4):
                    alternate(i, k, C_CONV, S_CONV, bhi, blo, (opnd_lo, KT) if k == 0 else None)

            def double(i, k, c0, s0, xhi, xlo, made):
                w = ring(i, 4, c0 + k)
                s = k // 2
                if k % 2 == 0:
                    free(s, i + s0)
                arrive = (made[0], made[1] + KT * k) if k < 2 else None
                product(s, w, xhi, xlo, k % 2 == 0, k % 2 == 1, KT * (k % 2), arrive).then_inc(chunk_done, 1)

            with pe.Fori(0, KT // 2) as i:
                for k in range(4):
                    double(i, k, C_MEM, S_MEM, mhi, mlo, (mem_lo, 0))
            with pe.Fori(0, KT // 4) as i:
                for k in range(4):
                    alternate(i, k, C_OUT, S_OUT, bhi, blo, (opnd_lo, 2 * KT) if k == 0 else None)
            pe.wait_ge(sq_added, 3 * KT)
            column_sums(sqs, 0).then_inc(stat_ready, 1)
            pe.wait_ge(root_ready, 3)
            sum_of_squares(3 * KT)
            for f in range(2):
                cf = C_FF + PERHALF * f
                sf = S_FF + S_HALF * f
                if f == 0:
                    ring(0, 4, cf + 1)
                    for s in range(2):
                        free(s, sf)
                    two_products(ahi, alo, 3 * KT)
                    for k in range(2, 4):
                        alternate(0, k, cf, sf, ahi, alo)
                with pe.Fori(1 - f, HID // 4) as i:
                    for k in range(4):
                        alternate(i, k, cf, sf, ahi, alo)
                with pe.Fori(0, KT // 2) as i:
                    for k in range(4):
                        double(i, k, cf + HID, sf + HID // 2, hidhi, hidlo, (hid_lo, HID * f))
            pe.wait_ge(sq_added, 5 * KT)
            column_sums(sqs, 0).then_inc(stat_ready, 1)


def kernel(x_prompt, x_sample, state_conv, state_C, state_n, state_m, g_pre_mix, w_in, b_in, w_dw, b_dw, g_cln, b_cln,
           w_conv_out, g_mh, w_m_out, w_o, g_post_mix, g_pre_ff, w_ff1, b_ff1, w_ff2, b_ff2, g_post_ff):
    import numpy as np
    import concourse.bacc as bacc
    from concourse.bass_utils import run_bass_kernel_spmd

    arr = lambda a: np.asarray(a)
    w, bi = arr(w_in)[0], arr(b_in)[0]
    o_ua, o_ug, o_q, o_k, o_v = 0, 1024, 2048, 3072, 4096
    o_o, o_ig, o_fg, o_gc, o_gm = 6144, 8192, 8196, 8200, 9224

    def chunks(m, rows=0):
        m = m[rows:rows + D_MODEL]
        return m.reshape(KT, P, m.shape[1] // P, P).transpose(2, 1, 0, 3)

    pair = lambda a, b: np.stack([a, b], axis=1).reshape((-1,) + a.shape[1:])
    parts = [pair(chunks(w[:, o_ug:o_q]), chunks(w[:, o_ua:o_ug]))]
    for h in range(HEADS):
        parts += [chunks(w[:, o_q + DK * h:o_q + DK * (h + 1)]), chunks(w[:, o_k + DK * h:o_k + DK * (h + 1)]),
                  chunks(w[:, o_v + DV * h:o_v + DV * (h + 1)]), chunks(w[:, o_o + DV * h:o_o + DV * (h + 1)])]
    parts += [chunks(w[:, o_gm:o_gm + D_MODEL]), chunks(w[:, o_gc:o_gm]), chunks(arr(w_conv_out)[0])]
    mo = arr(w_m_out)[0]
    parts += [pair(chunks(mo), chunks(mo, D_MODEL)), chunks(arr(w_o)[0])]
    ff1, ff2 = arr(w_ff1)[0], arr(w_ff2)[0]
    for f in range(2):
        parts += [chunks(ff1[:, HID * P * f:HID * P * (f + 1)]),
                  pair(chunks(ff2, HID * P * f), chunks(ff2, HID * P * f + D_MODEL))]
    wstream = np.concatenate(parts)

    feat = lambda v: v.reshape(-1, P).T
    cols = np.concatenate([feat(v) for v in (
        bi[o_ug:o_q], bi[o_ua:o_ug], bi[o_q:o_k], bi[o_k:o_v], bi[o_o:o_ig], bi[o_gc:o_gm], bi[o_gm:],
        arr(b_dw)[0], arr(g_cln)[0], arr(b_cln)[0], arr(g_pre_mix)[0], arr(g_mh)[0], arr(g_post_mix)[0],
        arr(g_pre_ff)[0], arr(b_ff1)[0], arr(b_ff2)[0], arr(g_post_ff)[0])], axis=1)
    w_gates = np.zeros((P, KT, 36), np.float32)
    w_gates[:, :, 0:4] = w[:, o_ig:o_fg].reshape(KT, P, 4).transpose(1, 0, 2)
    w_gates[:, :, 32:36] = w[:, o_fg:o_gc].reshape(KT, P, 4).transpose(1, 0, 2)
    b_gates = np.zeros((36, 1), np.float32)
    b_gates[0:4, 0] = bi[o_ig:o_fg]
    b_gates[32:36, 0] = bi[o_fg:o_gc]
    tokens = np.concatenate([arr(x_prompt)[0], arr(x_sample).reshape(NS, D_MODEL)])
    ins = dict(
        xT=tokens.T.reshape(KT, P, TT).transpose(1, 0, 2), wstream=wstream, w_gates=w_gates, cols=cols, b_gates=b_gates,
        b_v=bi[o_v:o_o].reshape(HEADS, DV), w_dw=arr(w_dw)[0].T.reshape(KT, P, WIDTH).transpose(1, 0, 2),
        hist=arr(state_conv)[0].transpose(2, 0, 1).reshape(KT, P, DEC_B, HIST).transpose(1, 0, 2, 3),
        c_in=arr(state_C)[0].transpose(1, 0, 3, 2).reshape(HEADS * DEC_B, QT, P, DV).transpose(0, 2, 1, 3),
        n_in=arr(state_n)[0].reshape(DEC_B, HEADS, QT, P).transpose(3, 1, 2, 0),
        m_in=arr(state_m)[0].T)
    outs = dict(yT=(P, KT, TT), conv_p=(P, KT, HIST), conv_s=(P, KT, DEC_B, HIST), c_p=(HEADS, VT, P, DK), n_p=(P, HEADS, QT),
                m_p=(HEADS, 1), c_s=(HEADS * DEC_B, P, QT, DV), n_s=(P, HEADS, QT, DEC_B), m_s=(HEADS, NS))

    nc = bacc.Bacc("TRN2", target_bir_lowering=False, num_devices=1, dynamic_dma_scratch_size=4096)
    arrays, aps = {}, {}
    for name, a in ins.items():
        arrays["in_" + name] = np.ascontiguousarray(a)
        aps[name] = nc.dram_tensor("in_" + name, a.shape, mybir.dt.float32, kind="ExternalInput").ap()
    for name, shape in outs.items():
        aps[name] = nc.dram_tensor("out_" + name, shape, mybir.dt.float32, kind="ExternalOutput").ap()
    hybrid_layer(nc, **aps)
    r = run_bass_kernel_spmd(nc, [arrays], core_ids=[0]).results[0]
    got = {name: np.asarray(r["out_" + name]) for name in outs}

    y = got["yT"].transpose(1, 0, 2).reshape(D_MODEL, TT).T
    conv_of_p = got["conv_p"].transpose(2, 1, 0).reshape(1, 1, HIST, D_MODEL)
    conv_of_s = got["conv_s"].transpose(2, 3, 1, 0).reshape(1, DEC_B, HIST, D_MODEL)
    c_of_s = got["c_s"].transpose(0, 2, 1, 3).reshape(HEADS, DEC_B, DK, DV).transpose(1, 0, 3, 2)
    return (y[:SEQ].reshape(1, SEQ, D_MODEL), y[SEQ:].reshape(DEC_B, DEC_T, D_MODEL),
            conv_of_p, got["c_p"].reshape(1, 1, HEADS, DV, DK), got["n_p"].transpose(1, 2, 0).reshape(1, 1, HEADS, DK),
            got["m_p"].reshape(1, 1, HEADS), conv_of_s, c_of_s.reshape(1, DEC_B, HEADS, DV, DK),
            got["n_s"].transpose(3, 1, 2, 0).reshape(1, DEC_B, HEADS, DK), got["m_s"][:, DEC_T - 1::DEC_T].T.reshape(1, DEC_B, HEADS))
```
